# Optimizing a Trainium2 kernel written in Bass

```python
import math
import jax, jax.numpy as jnp
from jax import lax
import numpy as np

D_MODEL = 1024
BATCH = 1
SEQ = 1024
DEPTH = 2
DEC_BATCH = 8
DEC_SEQ = 1
PAST_LEN = 2048
PAGE_SIZE = 128

N_MIXERS = 2
N_MLA_LAYERS = (DEPTH + N_MIXERS - 1) // N_MIXERS
N_SWA_LAYERS = DEPTH // N_MIXERS
NORM_EPS = 1e-6
NEG_INF = -1e30

MLA_HEADS = 16
Q_LORA = 512
KV_LORA = 256
QK_NOPE = 128
QK_ROPE = 64
V_HEAD = 128
ROPE_THETA = 10000.0
MLA_QBLOCK = 128
MLA_WIDTH = MLA_HEADS * V_HEAD
MLA_IN = Q_LORA + KV_LORA + QK_ROPE + MLA_WIDTH
MLA_SCALE = 1.0 / math.sqrt(QK_NOPE + QK_ROPE)

SWA_HEADS = 16
SWA_KV_HEADS = 4
SWA_GROUP = SWA_HEADS // SWA_KV_HEADS
SWA_HEAD_DIM = 64
WINDOW = 128
SWA_Q = SWA_HEADS * SWA_HEAD_DIM
SWA_KV = SWA_KV_HEADS * SWA_HEAD_DIM
SWA_IN = 2 * SWA_Q + 2 * SWA_KV
SWA_SCALE = 1.0 / math.sqrt(SWA_HEAD_DIM)

kernel_name = 'hybrid_mla_swa_sink_decoder_step'

def rmsnorm(x, g):
    xf = x.astype(jnp.float32)
    y = xf * lax.rsqrt(jnp.mean(xf * xf, axis=-1, keepdims=True) + NORM_EPS)
    return (y * g.astype(jnp.float32)).astype(x.dtype)

def rope_tables(pos):
    inv = ROPE_THETA ** (-jnp.arange(0, QK_ROPE, 2, dtype=jnp.float32) / QK_ROPE)
    ang = pos.astype(jnp.float32)[:, None] * inv[None, :]
    ang = jnp.concatenate([ang, ang], axis=-1)
    return jnp.cos(ang), jnp.sin(ang)

def apply_rope(x, cos, sin):
    xf = x.astype(jnp.float32)
    half = QK_ROPE // 2
    rot = jnp.concatenate([-xf[..., half:], xf[..., :half]], axis=-1)
    return (xf * cos + rot * sin).astype(x.dtype)

def alibi_slopes():
    h = jnp.arange(1, SWA_HEADS + 1, dtype=jnp.float32)
    return (2.0 ** (-8.0 * h / SWA_HEADS)).reshape(SWA_KV_HEADS, SWA_GROUP)

def gated_out(o, gate, w_o):
    return (o * jax.nn.silu(gate)) @ w_o

def mla_project(h, pos, w_in, q_norm, w_qb, kv_norm):
    z = h @ w_in
    cq = rmsnorm(z[..., :Q_LORA], q_norm)
    ckv = rmsnorm(z[..., Q_LORA:Q_LORA + KV_LORA], kv_norm)
    kpe = z[..., Q_LORA + KV_LORA:Q_LORA + KV_LORA + QK_ROPE]
    gate = z[..., Q_LORA + KV_LORA + QK_ROPE:]
    q = jnp.einsum('bsc,chd->bshd', cq, w_qb)
    q_nope, q_rope = q[..., :QK_NOPE], q[..., QK_NOPE:]
    cos, sin = rope_tables(pos)
    q_rope = apply_rope(q_rope, cos[:, None, :], sin[:, None, :])
    kpe = apply_rope(kpe, cos, sin)
    return q_nope, q_rope, ckv, kpe, gate

def mla_prompt_attention(q_nope, q_rope, ckv, kpe, w_uk, w_uv):
    b, s = q_nope.shape[:2]
    k_nope = jnp.einsum('bsc,chn->bshn', ckv, w_uk)
    v = jnp.einsum('bsc,chv->bshv', ckv, w_uv)
    nb = s // MLA_QBLOCK
    qn = q_nope.reshape(b, nb, MLA_QBLOCK, MLA_HEADS, QK_NOPE).swapaxes(0, 1)
    qr = q_rope.reshape(b, nb, MLA_QBLOCK, MLA_HEADS, QK_ROPE).swapaxes(0, 1)
    kpos = jnp.arange(s, dtype=jnp.int32)

    def block(args):
        qn_b, qr_b, blk = args
        sc = (jnp.einsum('bqhn,bkhn->bhqk', qn_b, k_nope)
              + jnp.einsum('bqhr,bkr->bhqk', qr_b, kpe)).astype(jnp.float32) * MLA_SCALE
        qpos = blk * MLA_QBLOCK + jnp.arange(MLA_QBLOCK, dtype=jnp.int32)
        sc = jnp.where(kpos[None, :] <= qpos[:, None], sc, NEG_INF)
        p = jax.nn.softmax(sc, axis=-1).astype(v.dtype)
        return jnp.einsum('bhqk,bkhv->bqhv', p, v)

    o = lax.map(block, (qn, qr, jnp.arange(nb, dtype=jnp.int32)))
    return o.swapaxes(0, 1).reshape(b, s, MLA_HEADS, V_HEAD)

def mla_sample_attention(q_nope, q_rope, ckv_new, kpe_new, past_ckv, past_kpe, w_uk, w_uv):
    t = q_nope.shape[1]
    past_len = past_ckv.shape[1]
    q_lat = jnp.einsum('bthn,chn->bthc', q_nope, w_uk)
    s_past = (jnp.einsum('bthc,bsc->bhts', q_lat, past_ckv)
              + jnp.einsum('bthr,bsr->bhts', q_rope, past_kpe)).astype(jnp.float32) * MLA_SCALE
    s_new = (jnp.einsum('bthc,buc->bhtu', q_lat, ckv_new)
             + jnp.einsum('bthr,bur->bhtu', q_rope, kpe_new)).astype(jnp.float32) * MLA_SCALE
    causal = jnp.arange(t)[None, :] <= jnp.arange(t)[:, None]
    s_new = jnp.where(causal, s_new, NEG_INF)
    p = jax.nn.softmax(jnp.concatenate([s_past, s_new], axis=-1), axis=-1).astype(ckv_new.dtype)
    o_lat = (jnp.einsum('bhts,bsc->bthc', p[..., :past_len], past_ckv)
             + jnp.einsum('bhtu,buc->bthc', p[..., past_len:], ckv_new))
    return jnp.einsum('bthc,chv->bthv', o_lat, w_uv)

def swa_project(h, w_in):
    b, s = h.shape[:2]
    z = h @ w_in
    q = z[..., :SWA_Q].reshape(b, s, SWA_KV_HEADS, SWA_GROUP, SWA_HEAD_DIM)
    k = z[..., SWA_Q:SWA_Q + SWA_KV].reshape(b, s, SWA_KV_HEADS, SWA_HEAD_DIM)
    v = z[..., SWA_Q + SWA_KV:SWA_Q + 2 * SWA_KV].reshape(b, s, SWA_KV_HEADS, SWA_HEAD_DIM)
    gate = z[..., SWA_Q + 2 * SWA_KV:]
    return q, k, v, gate

def sink_softmax(sc, valid, sinks):
    sc = jnp.where(valid, sc, NEG_INF)
    sk = sinks.astype(jnp.float32).reshape(SWA_KV_HEADS, SWA_GROUP)[:, :, None, None]
    m = jnp.maximum(jnp.max(sc, axis=-1, keepdims=True), sk)
    e = jnp.exp(sc - m)
    return e / (jnp.sum(e, axis=-1, keepdims=True) + jnp.exp(sk - m))

def swa_prompt_attention(q, k, v, sinks):
    b, s = q.shape[:2]
    nb = s // WINDOW
    qb = q.reshape(b, nb, WINDOW, SWA_KV_HEADS, SWA_GROUP, SWA_HEAD_DIM)
    kb = k.reshape(b, nb, WINDOW, SWA_KV_HEADS, SWA_HEAD_DIM)
    vb = v.reshape(b, nb, WINDOW, SWA_KV_HEADS, SWA_HEAD_DIM)
    kk = jnp.concatenate([jnp.concatenate([jnp.zeros_like(kb[:, :1]), kb[:, :-1]], axis=1), kb], axis=2)
    vv = jnp.concatenate([jnp.concatenate([jnp.zeros_like(vb[:, :1]), vb[:, :-1]], axis=1), vb], axis=2)
    sc = jnp.einsum('bnqkgd,bnskd->bnkgqs', qb, kk).astype(jnp.float32) * SWA_SCALE
    qi = WINDOW + jnp.arange(WINDOW)
    ki = jnp.arange(2 * WINDOW)
    dist = qi[:, None] - ki[None, :]
    in_win = (dist >= 0) & (dist < WINDOW)
    blk_ok = (jnp.arange(nb)[:, None] > 0) | (ki[None, :] >= WINDOW)
    valid = in_win[None] & blk_ok[:, None, :]
    sc = sc - alibi_slopes()[:, :, None, None] * dist.astype(jnp.float32)
    p = sink_softmax(sc, valid[None, :, None, None], sinks).astype(v.dtype)
    o = jnp.einsum('bnkgqs,bnskd->bnqkgd', p, vv)
    return o.reshape(b, s, SWA_Q)

def swa_sample_attention(q, k, v, buf_k, buf_v, sinks, past_len):
    b, t = q.shape[:2]
    nbuf = buf_k.shape[1]
    kk = jnp.concatenate([buf_k, k], axis=1)
    vv = jnp.concatenate([buf_v, v], axis=1)
    kpos = past_len - nbuf + jnp.arange(nbuf + t)
    qpos = past_len + jnp.arange(t)
    dist = qpos[:, None] - kpos[None, :]
    valid = (dist >= 0) & (dist < WINDOW)
    sc = jnp.einsum('btkgd,bskd->bkgts', q, kk).astype(jnp.float32) * SWA_SCALE
    sc = sc - alibi_slopes()[:, :, None, None] * dist.astype(jnp.float32)
    p = sink_softmax(sc, valid, sinks).astype(v.dtype)
    o = jnp.einsum('bkgts,bskd->btkgd', p, vv)
    return o.reshape(b, t, SWA_Q), kk[:, t:], vv[:, t:]

def setup_inputs(seed: int = 0) -> dict:
    key = jax.random.key(seed)
    ks = jax.random.split(key, 24)
    n_pages = PAST_LEN // PAGE_SIZE
    n_used = DEC_BATCH * n_pages
    n_phys = (5 * n_used + 3) // 4
    swa_buf = min(WINDOW, PAST_LEN)

    def nrm(k, shape, scale=1.0):
        return jax.random.normal(k, shape, jnp.float32) * scale

    def gain(k, shape):
        return 1.0 + 0.05 * jax.random.normal(k, shape, jnp.float32)

    perm = jax.random.permutation(ks[0], n_phys)
    page_table = perm[:n_used].reshape(DEC_BATCH, n_pages).astype(jnp.int32)
    return {
        'x_prompt': nrm(ks[1], (BATCH, SEQ, D_MODEL)),
        'x_sample': nrm(ks[2], (DEC_BATCH, DEC_SEQ, D_MODEL)),
        'cache_ckv': nrm(ks[3], (N_MLA_LAYERS, n_phys, PAGE_SIZE, KV_LORA)),
        'cache_kpe': nrm(ks[4], (N_MLA_LAYERS, n_phys, PAGE_SIZE, QK_ROPE)),
        'state_swa_k': nrm(ks[5], (N_SWA_LAYERS, DEC_BATCH, swa_buf, SWA_KV_HEADS, SWA_HEAD_DIM)),
        'state_swa_v': nrm(ks[6], (N_SWA_LAYERS, DEC_BATCH, swa_buf, SWA_KV_HEADS, SWA_HEAD_DIM)),
        'page_table': page_table,
        'pre_norm': gain(ks[7], (DEPTH, D_MODEL)),
        'post_norm': gain(ks[8], (DEPTH, D_MODEL)),
        'mla_w_in': nrm(ks[9], (N_MLA_LAYERS, D_MODEL, MLA_IN), D_MODEL ** -0.5),
        'mla_q_norm': gain(ks[10], (N_MLA_LAYERS, Q_LORA)),
        'mla_w_qb': nrm(ks[11], (N_MLA_LAYERS, Q_LORA, MLA_HEADS, QK_NOPE + QK_ROPE), Q_LORA ** -0.5),
        'mla_kv_norm': gain(ks[12], (N_MLA_LAYERS, KV_LORA)),
        'mla_w_uk': nrm(ks[13], (N_MLA_LAYERS, KV_LORA, MLA_HEADS, QK_NOPE), KV_LORA ** -0.5),
        'mla_w_uv': nrm(ks[14], (N_MLA_LAYERS, KV_LORA, MLA_HEADS, V_HEAD), KV_LORA ** -0.5),
        'mla_w_o': nrm(ks[15], (N_MLA_LAYERS, MLA_WIDTH, D_MODEL), MLA_WIDTH ** -0.5),
        'swa_w_in': nrm(ks[16], (N_SWA_LAYERS, D_MODEL, SWA_IN), D_MODEL ** -0.5),
        'swa_sinks': nrm(ks[17], (N_SWA_LAYERS, SWA_HEADS)),
        'swa_w_o': nrm(ks[18], (N_SWA_LAYERS, SWA_Q, D_MODEL), SWA_Q ** -0.5),
    }

def reference(x_prompt, x_sample, cache_ckv, cache_kpe, state_swa_k, state_swa_v, page_table,
              pre_norm, post_norm, mla_w_in, mla_q_norm, mla_w_qb, mla_kv_norm, mla_w_uk,
              mla_w_uv, mla_w_o, swa_w_in, swa_sinks, swa_w_o):
    n_b, seq, _ = x_prompt.shape
    n_db, t_new, _ = x_sample.shape
    past_len = page_table.shape[1] * PAGE_SIZE
    pos_p = jnp.arange(seq, dtype=jnp.int32)
    pos_s = past_len + jnp.arange(t_new, dtype=jnp.int32)
    hp, hs = x_prompt, x_sample
    ckv_p, kpe_p, ckv_s, kpe_s = [], [], [], []
    swk_p, swv_p, swk_s, swv_s = [], [], [], []
    for i in range(DEPTH):
        ap = rmsnorm(hp, pre_norm[i])
        a_s = rmsnorm(hs, pre_norm[i])
        l = i // N_MIXERS
        if i % N_MIXERS == 0:
            qn, qr, ckv, kpe, gate = mla_project(ap, pos_p, mla_w_in[l], mla_q_norm[l],
                                                 mla_w_qb[l], mla_kv_norm[l])
            o = mla_prompt_attention(qn, qr, ckv, kpe, mla_w_uk[l], mla_w_uv[l])
            mp = gated_out(o.reshape(n_b, seq, MLA_WIDTH), gate, mla_w_o[l])
            ckv_p.append(ckv)
            kpe_p.append(kpe)
            qn, qr, ckv, kpe, gate = mla_project(a_s, pos_s, mla_w_in[l], mla_q_norm[l],
                                                 mla_w_qb[l], mla_kv_norm[l])
            past_ckv = cache_ckv[l, page_table].reshape(n_db, past_len, KV_LORA)
            past_kpe = cache_kpe[l, page_table].reshape(n_db, past_len, QK_ROPE)
            o = mla_sample_attention(qn, qr, ckv, kpe, past_ckv, past_kpe, mla_w_uk[l], mla_w_uv[l])
            ms = gated_out(o.reshape(n_db, t_new, MLA_WIDTH), gate, mla_w_o[l])
            ckv_s.append(ckv)
            kpe_s.append(kpe)
        else:
            q, k, v, gate = swa_project(ap, swa_w_in[l])
            o = swa_prompt_attention(q, k, v, swa_sinks[l])
            mp = gated_out(o, gate, swa_w_o[l])
            keep = min(WINDOW, seq)
            swk_p.append(k[:, seq - keep:])
            swv_p.append(v[:, seq - keep:])
            q, k, v, gate = swa_project(a_s, swa_w_in[l])
            o, nk, nv = swa_sample_attention(q, k, v, state_swa_k[l], state_swa_v[l],
                                             swa_sinks[l], past_len)
            ms = gated_out(o, gate, swa_w_o[l])
            swk_s.append(nk)
            swv_s.append(nv)
        hp = hp + rmsnorm(mp, post_norm[i])
        hs = hs + rmsnorm(ms, post_norm[i])
    return (hp, hs, jnp.stack(ckv_p), jnp.stack(kpe_p), jnp.stack(ckv_s), jnp.stack(kpe_s),
            jnp.stack(swk_p), jnp.stack(swv_p), jnp.stack(swk_s), jnp.stack(swv_s))


_drawn_inputs = setup_inputs


def setup_inputs(seed=0):
    import zlib

    import numpy as np

    out = dict(_drawn_inputs(seed))
    spreads = {}
    factors = {}
    for name, (base, spread) in spreads.items():
        noise = np.random.default_rng([zlib.crc32(name.encode()), seed]).standard_normal(out[name].shape)
        drawn = base * np.exp(spread * noise) if base else spread * noise
        out[name] = __import__('jax').numpy.asarray(drawn.astype(out[name].dtype))
    for name, factor in factors.items():
        out[name] = (out[name] * factor).astype(out[name].dtype)
    return out
```

```python
from contextlib import ExitStack

import concourse.bass as bass
from concourse import mybir

P = 128
D = 1024
SEQ, DEC = 1024, 8
TOK = SEQ + DEC
NT = SEQ // P
KT = D // P
CH = TOK // 3
H = 16
QL, KVL, ROPE, NOPE = 512, 256, 64, 128
PAST, PAGE = 2048, 128
NPG = PAST // PAGE
EPS = 1e-6
MLA_SCALE = float((NOPE + ROPE) ** -0.5)
SWA_SCALE = 0.125
QW = 4 * 256
HWC = QW + 2 * 2 * P
PGW = KVL + ROPE
N_Z = 7
N_MIN, N_MO, N_SIN, N_SO = N_Z + H, 16, 20, 8
B_MO = N_MIN
B_SIN = B_MO + N_MO
B_SO = B_SIN + N_SIN

F32 = mybir.dt.float32
R32 = mybir.dt.float32r
I32 = mybir.dt.int32
ACT = mybir.ActivationFunctionType
ALU = mybir.AluOpType
AX = mybir.AxisListType
ds = bass.ds


def due(value):
    return not isinstance(value, int) or value > 0


def pairs(eng, n, body):
    body(0)
    if n > 1:
        with eng.Fori(1, n) as i:
            body(i)


class Weights:

    def __init__(self, nc, st, tag):
        self.raw = st.enter_context(nc.sbuf_tensor(f"w_raw_{tag}", [P, 2, D], F32))
        self.hi = st.enter_context(nc.sbuf_tensor(f"w_hi_{tag}", [P, 2, D], R32))
        self.lo = st.enter_context(nc.sbuf_tensor(f"w_lo_{tag}", [P, 2, D], R32))
        self.landed = [st.enter_context(nc.semaphore(f"w_landed{u}_{tag}")) for u in range(2)]
        self.rounded = st.enter_context(nc.semaphore(f"w_rounded_{tag}"))
        self.split = st.enter_context(nc.semaphore(f"w_split_{tag}"))
        self.used = st.enter_context(nc.semaphore(f"w_used_{tag}"))


def load_weights(nc, sp, w, tiles, base, n):
    def load(i, u):
        if due(2 * i + u - 1):
            sp.wait_ge(w.split, 2 * i + u - 1)
        nc.sync.dma_start(w.raw[:, u, :], tiles[ds(base + 2 * i + u, 1)].rearrange("a p c -> (a p) c")
                          ).then_inc(w.landed[u], 16)

    pairs(sp, n // 2, lambda i: [load(i, u) for u in range(2)])
    if n % 2:
        load(n // 2, 0)


def split_weights(nc, pool, w, ones, n):
    def split(i, u):
        if due(2 * i + u - 1):
            pool.wait_ge(w.used, 2 * i + u - 1)
        pool.wait_ge(w.landed[u], 16 * (i + 1))
        nc.gpsimd.tensor_tensor(w.hi[:, u, :], w.raw[:, u, :], ones[:, 0:1].to_broadcast([P, D]),
                                ALU.mult).then_inc(w.rounded, 1)
        pool.wait_ge(w.rounded, 2 * i + u + 1)
        nc.gpsimd.tensor_tensor(w.lo[:, u, :], w.raw[:, u, :], w.hi[:, u, :].bitcast(F32),
                                ALU.subtract).then_inc(w.split, 1)

    pairs(pool, n // 2, lambda i: [split(i, u) for u in range(2)])
    if n % 2:
        split(n // 2, 0)


def job_matmuls(nc, w, slot, ps, bank, xh, xl, k0, start, stop):
    for k in range(KT):
        first, last = start and k == 0, stop and k == KT - 1
        wh, wl = w.hi[:, slot, k * P:(k + 1) * P], w.lo[:, slot, k * P:(k + 1) * P]
        for x, (wt, xt) in enumerate(((wh, xh), (wh, xl), (wl, xh))):
            for c in range(3):
                mm = nc.tensor.matmul(ps[:, bank + c, 0:CH], wt, xt[:, k0 + k, c * CH:(c + 1) * CH],
                                      start=first and x == 0, stop=last and x == 2)
    return mm


def psum3(ps, u):
    return ps[:, 3 * u:3 * u + 3, 0:CH]


def chunks(row):
    return row.rearrange("p (c n) -> p c n", c=3)


def phase_mla_in(nc, a, g):
    ps = g.ps
    with ExitStack() as st:
        def sb(name, shape, dt=F32):
            return st.enter_context(nc.sbuf_tensor(name, shape, dt))

        def sem(name):
            return st.enter_context(nc.semaphore(name))

        w = Weights(nc, st, "a")
        xh, xl = sb("a_xh", [P, KT, TOK], R32), sb("a_xl", [P, KT, TOK], R32)
        z = sb("a_z", [P, N_Z, TOK])
        work = g.cq_alias
        x_t, x_s, x_g = (work[:, 2 * j * D:(2 * j + 2) * D].rearrange("p (u n) -> p u n", u=2) for j in range(3))
        junk = work[:, 6 * D:7 * D]
        stage = sb("a_stage", [P, 2, TOK])
        root = sb("a_root", [P, 2, TOK])
        tok_out = sb("a_tok_out", [P, 2, PGW])
        stat = sb("a_stat", [P, 2, 3])
        consts_in, consts_made = sem("a_consts_in"), sem("a_consts_made")
        x_in = [sem(f"a_x_in{u}") for u in range(2)]
        squared, rooted, inverted, scaled = sem("a_squared"), sem("a_rooted"), sem("a_inverted"), sem("a_scaled")
        turned, gained, x_hi, x_lo = sem("a_turned"), sem("a_gained"), sem("a_x_hi"), sem("a_x_lo")
        job_read = sem("a_job_read")
        silu, gate_kept = sem("a_silu"), sem("a_gate_kept")
        gate_out = [sem(f"a_gate_out{u}") for u in range(2)]
        z_sq, ss_done, ss_root, ss_inv = sem("a_z_sq"), sem("a_ss_done"), sem("a_ss_root"), sem("a_ss_inv")
        z_norm, z_hi, z_lo = sem("a_z_norm"), sem("a_z_hi"), sem("a_z_lo")
        kr_mul, kr_add, kr_hi, kr_lo = sem("a_kr_mul"), sem("a_kr_add"), sem("a_kr_hi"), sem("a_kr_lo")
        tok_turned, tok_copied = sem("a_tok_turned"), sem("a_tok_copied")
        tok_stored = [sem(f"a_tok_stored{u}") for u in range(2)]
        kept = sem("a_kept")
        sq_flat = work
        kr = sb("a_kr", [ROPE, 2, TOK])
        block = st.enter_context(nc.Block())

        @block.sync
        def _(sp):
            for dst, src in ((g.ident, a["ident"]), (g.gains, a["gains"]), (g.cs, a["cs"])):
                nc.sync.dma_start(dst[:], src).then_inc(consts_in, 16)
            def load_x(i):
                for u in range(2):
                    if due(2 * i + u - 1):
                        sp.wait_ge(scaled, 2 * i + u - 1)
                    nc.sync.dma_start(x_t[:, u, :], a["x_prompt"][ds((2 * i + u) * P, P), :]).then_inc(x_in[u], 16)
            pairs(sp, NT // 2, load_x)
            sp.wait_ge(scaled, NT - 1)
            nc.sync.dma_start(x_t[0:DEC, 0, :], a["x_sample"]).then_inc(x_in[0], 16)
            load_weights(nc, sp, w, a["w_tiles"], 0, N_MIN)

        @block.gpsimd
        def _(pool):
            nc.gpsimd.memset(g.ones[:], 1.0).then_inc(consts_made, 1)
            nc.gpsimd.memset(g.eps[:], EPS).then_inc(consts_made, 1)
            pool.wait_ge(consts_made, 2)

            def x_low(i, u, rows=P):
                t = 2 * i + u
                pool.wait_ge(x_hi, t + 1)
                nc.gpsimd.tensor_tensor(xl[:, :, ds(t * P, rows)],
                                        x_g[:, u, :].rearrange("p (k n) -> p k n", k=KT)[:, :, 0:rows],
                                        xh[:, :, ds(t * P, rows)].bitcast(F32), ALU.subtract).then_inc(x_lo, 1)
            pairs(pool, NT // 2, lambda i: [x_low(i, u) for u in range(2)])
            x_low(NT // 2, 0, DEC)
            split_weights(nc, pool, w, g.ones, N_MIN)

        @block.scalar
        def _(act):
            act.wait_ge(consts_made, 2)
            act.wait_ge(consts_in, 48)
            nc.scalar.activation(g.identr[:], g.ident[:], ACT.Copy).then_inc(kept, 1)

            def statistics(i, u, rows=P):
                t = 2 * i + u
                act.wait_ge(x_in[u], 16 * (i + 1))
                nc.scalar.activation(junk[0:rows], x_t[0:rows, u, :], ACT.Square,
                                     accum_out=stat[0:rows, u, 0:1]).then_inc(squared, 1)
                act.wait_ge(squared, t + 1)
                if due(t - 1):
                    act.wait_ge(inverted, t - 1)
                nc.scalar.activation(stat[0:rows, u, 1:2], stat[0:rows, u, 0:1], ACT.Sqrt, scale=1.0 / D,
                                     bias=g.eps[0:rows]).then_inc(rooted, 1)

            def x_high(i, u, rows=P):
                t = 2 * i + u
                act.wait_ge(gained, t + 1)
                nc.scalar.activation(xh[:, :, ds(t * P, rows)],
                                     x_g[:, u, :].rearrange("p (k n) -> p k n", k=KT)[:, :, 0:rows],
                                     ACT.Copy).then_inc(x_hi, 1)
            def both(i):
                statistics(i, 0)
                statistics(i, 1)
                x_high(i, 0)
                x_high(i, 1)
            pairs(act, NT // 2, both)
            statistics(NT // 2, 0, DEC)
            x_high(NT // 2, 0, DEC)

            def latent(j):
                act.wait_ge(w.used, j + 1)
                nc.scalar.activation(chunks(z[:, j, :]), psum3(ps, j % 2), ACT.Copy).then_inc(job_read, 1)
                if j < N_Z - 1:
                    act.wait_ge(job_read, j + 1)
                    act.wait_ge(x_lo, NT + 1)
                    nc.scalar.activation(sq_flat[:, j * TOK:(j + 1) * TOK], z[:, j, :], ACT.Square).then_inc(z_sq, 1)

            def gate(i, v):
                h = 2 * i + v
                act.wait_ge(w.used, N_Z + h + 1)
                if due(16 * i):
                    act.wait_ge(gate_out[v], 16 * i)
                if due(h - 1):
                    act.wait_ge(gate_kept, h - 1)
                nc.scalar.activation(chunks(stage[:, v, :]), psum3(ps, (N_Z + v) % 2), ACT.Silu).then_inc(job_read, 1)
                act.wait_ge(job_read, N_Z + h + 1)
                nc.scalar.dma_start(g.gate_dram[ds(h, 1)].rearrange("a p n -> (a p) n"), stage[:, v, 0:SEQ]
                                    ).then_inc(gate_out[v], 16)
                nc.scalar.activation(g.gate_s[:, ds(h, 1), :].rearrange("p a n -> p (a n)"), stage[:, v, SEQ:TOK],
                                     ACT.Copy).then_inc(gate_kept, 1)

            for j in range(N_Z):
                latent(j)
            gate(0, 0)
            gate(0, 1)
            for c in range(6):
                act.wait_ge(ss_done, c + 1)
                width = QL if c < 3 else KVL
                nc.scalar.activation(root[:, c // 3, (c % 3) * CH:(c % 3 + 1) * CH], ps[:, 6 + c % 2, 0:CH],
                                     ACT.Sqrt, scale=1.0 / width, bias=g.eps[:]).then_inc(ss_root, 1)
            for h in range(2, 6):
                gate(h // 2, h % 2)
                for j in {2: (0, 1), 3: (2, 3), 4: (4, 5), 5: ()}[h]:
                    act.wait_ge(z_norm, j + 1)
                    dst, src = (g.cqh[:, j, :], z[:, j, :]) if j < 4 else (g.ckvh[:, j - 4, :], z[:, j, 0:SEQ])
                    nc.scalar.activation(dst, src, ACT.Copy).then_inc(z_hi, 1)
                if h == 5:
                    act.wait_ge(kr_add, 1)
                    nc.scalar.activation(g.krh[0:ROPE, :], kr[:, 0, 0:SEQ], ACT.Copy).then_inc(kr_hi, 1)
                    nc.scalar.activation(g.krh[ROPE:P, :], kr[:, 0, 0:SEQ], ACT.Copy).then_inc(kr_hi, 1)
                    nc.scalar.activation(g.ckv_s[0:ROPE, 2, :], kr[:, 0, SEQ:TOK], ACT.Copy).then_inc(kept, 1)
                    for j in range(2):
                        nc.scalar.activation(g.ckv_s[:, j, :], z[:, 4 + j, SEQ:TOK], ACT.Copy).then_inc(kept, 1)
            with act.Fori(3, 6) as i:
                gate(i, 0)
                gate(i, 1)

            def tokens_out(t):
                rows = P if t < NT else DEC
                u = t % 2
                act.wait_ge(tok_copied, t + 1)
                to = (a["new_ckv_prompt"][0, 0, t * P:(t + 1) * P, :], a["new_kpe_prompt"][0, 0, t * P:(t + 1) * P, :]) \
                    if t < NT else (a["new_ckv_sample"][0, :, 0, :], a["new_kpe_sample"][0, :, 0, :])
                nc.scalar.dma_start(to[0], tok_out[0:rows, u, 0:KVL]).then_inc(tok_stored[u], 16)
                nc.scalar.dma_start(to[1], tok_out[0:rows, u, KVL:PGW]).then_inc(tok_stored[u], 16)
            for h in range(12, H):
                for t in range(3 * (h - 12), min(3 * (h - 11), NT + 1)):
                    tokens_out(t)
                gate(h // 2, h % 2)
            for u in range(2):
                act.wait_ge(gate_out[u], 16 * (H // 2))
                act.wait_ge(tok_stored[u], 32 * (5 - u))

        @block.vector
        def _(dve):
            dve.wait_ge(consts_in, 48)

            def scale_rows(i, u, rows=P):
                t = 2 * i + u
                dve.wait_ge(rooted, t + 1)
                nc.vector.reciprocal(stat[0:rows, u, 2:3], stat[0:rows, u, 1:2]).then_inc(inverted, 1)
                dve.wait_ge(inverted, t + 1)
                if due(t - 1):
                    dve.wait_ge(turned, t - 1)
                nc.vector.tensor_scalar(x_s[0:rows, u, :], x_t[0:rows, u, :], stat[0:rows, u, 2:3], None,
                                        ALU.mult).then_inc(scaled, 1)

            def apply_gain(i, u, rows=P):
                t = 2 * i + u
                dve.wait_ge(turned, t + 1)
                if due(t - 1):
                    dve.wait_ge(x_lo, t - 1)
                nc.vector.tensor_tensor(x_g[:, u, :].rearrange("p (k n) -> p k n", k=KT)[:, :, 0:rows],
                                        ps[:, 2 * u:2 * u + 2, :].rearrange("p b (k n) -> p (b k) n", k=4)[:, :, 0:rows],
                                        g.gains[:, 0:KT].unsqueeze(2).to_broadcast([P, KT, rows]),
                                        ALU.mult).then_inc(gained, 1)
            def both(i):
                scale_rows(i, 0)
                scale_rows(i, 1)
                apply_gain(i, 0)
                apply_gain(i, 1)
            pairs(dve, NT // 2, both)
            scale_rows(NT // 2, 0, DEC)
            apply_gain(NT // 2, 0, DEC)

            dve.wait_ge(job_read, N_Z)
            nc.vector.tensor_tensor(kr[:, 0, :], z[0:ROPE, 6, :], g.cs[0:ROPE, :], ALU.mult).then_inc(kr_mul, 1)
            nc.vector.tensor_tensor(kr[:, 1, :], z[ROPE:P, 6, :], g.cs[ROPE:P, :], ALU.mult).then_inc(kr_mul, 1)
            dve.wait_ge(kr_mul, 2)
            nc.vector.tensor_tensor(kr[:, 0, :], kr[:, 0, :], kr[:, 1, :], ALU.add).then_inc(kr_add, 1)
            for f in range(2):
                dve.wait_ge(ss_root, 3 * (f + 1))
                nc.vector.reciprocal(root[:, f, :], root[:, f, :]).then_inc(ss_inv, 1)
            for j in range(6):
                dve.wait_ge(ss_inv, 1 + (j >= 4))
                dve.wait_ge(z_sq, 6)
                nc.vector.scalar_tensor_tensor(out=z[:, j, :], in0=z[:, j, :], scalar=g.gains[:, 16 + j:17 + j],
                                               in1=root[:, j // 4, :], op0=ALU.mult, op1=ALU.mult).then_inc(z_norm, 1)
            for j in range(6):
                hi, lo = (g.cqh[:, j, :], g.cql[:, j, :]) if j < 4 else (g.ckvh[:, j - 4, :], g.ckvl[:, j - 4, :])
                dve.wait_ge(z_hi, j + 1)
                nc.vector.tensor_tensor(lo, z[:, j, 0:TOK if j < 4 else SEQ], hi.bitcast(F32),
                                        ALU.subtract).then_inc(z_lo, 1)
            dve.wait_ge(kr_hi, 2)
            nc.vector.tensor_tensor(g.krl[:, :], kr[:, 0, 0:SEQ], g.krh[0:ROPE, :].bitcast(F32),
                                    ALU.subtract).then_inc(kr_lo, 1)
            for t in range(NT + 1):
                rows, u = (P if t < NT else DEC), t % 2
                dve.wait_ge(tok_turned, t + 1)
                if due(32 * (t // 2)):
                    dve.wait_ge(tok_stored[u], 32 * (t // 2))
                nc.vector.tensor_copy(tok_out[0:rows, u, :], ps[0:rows, 6 + u, 0:PGW]).then_inc(tok_copied, 1)

        @block.tensor
        def _(pe):
            pe.wait_ge(consts_in, 48)

            def turn(i, u, rows=P):
                t = 2 * i + u
                pe.wait_ge(scaled, t + 1)
                if due(t - 1):
                    pe.wait_ge(gained, t - 1)
                for k in range(KT):
                    mm = nc.tensor.transpose(ps[:, 2 * u + k // 4, (k % 4) * P:(k % 4) * P + rows],
                                             x_s[0:rows, u, k * P:(k + 1) * P], g.ident[0:rows, 0:rows])
                mm.then_inc(turned, 1)
            pairs(pe, NT // 2, lambda i: [turn(i, u) for u in range(2)])
            turn(NT // 2, 0, DEC)
            pe.wait_ge(gained, NT + 1)
            pe.wait_ge(x_lo, NT + 1)
            pe.wait_ge(x_hi, NT + 1)

            def job(n, slot):
                pe.wait_ge(w.split, n + 1)
                if due(n - 1):
                    pe.wait_ge(job_read, n - 1)
                job_matmuls(nc, w, slot, ps, 3 * slot, xh, xl, 0, True, True).then_inc(w.used, 1)

            job(0, 0)
            job(1, 1)
            with pe.Fori(1, 3) as i:
                job(2 * i, 0)
                job(2 * i + 1, 1)
            for n in range(6, 9):
                job(n, n % 2)
            pe.wait_ge(z_sq, 6)
            for c in range(6):
                if due(c - 1):
                    pe.wait_ge(ss_root, c - 1)
                tiles = range(4) if c < 3 else range(4, 6)
                for j in tiles:
                    off = j * TOK + (c % 3) * CH
                    mm = nc.tensor.matmul(ps[:, 6 + c % 2, 0:CH], g.ones[:], sq_flat[:, off:off + CH],
                                          start=j == tiles[0], stop=j == tiles[-1])
                mm.then_inc(ss_done, 1)
            with pe.Fori(4, 9) as i:
                job(2 * i + 1, 1)
                job(2 * i + 2, 0)
            pe.wait_ge(z_norm, 6)
            pe.wait_ge(kr_add, 1)
            pe.wait_ge(ss_root, 6)
            for n in range(19, N_MIN):
                for t in range(3 * (n - 19), min(3 * (n - 18), NT + 1)):
                    rows, u = (P if t < NT else DEC), t % 2
                    if due(t - 1):
                        pe.wait_ge(tok_copied, t - 1)
                    for j in range(2):
                        nc.tensor.transpose(ps[0:rows, 6 + u, j * P:(j + 1) * P], z[:, 4 + j, t * P:t * P + rows], g.ident[:])
                    nc.tensor.transpose(ps[0:rows, 6 + u, KVL:PGW], kr[:, 0, t * P:t * P + rows],
                                        g.ident[0:ROPE, 0:ROPE]).then_inc(tok_turned, 1)
                job(n, n % 2)


PJ = [("qn", 0), ("qn", 1), ("qn", 2), ("qr", 0), ("qr", 1), ("qr", 2), ("k", 0), ("k", 1), ("v", 0), ("v", 1)]
N_PJ = len(PJ)
Q_TILES = NT
GRP = Q_TILES // 2
N_PT = sum(m + 1 for m in range(GRP))


N_BEFORE = [sum(k + 1 for k in range(m)) for m in range(GRP)]


def pt_bank(m, c):
    return 4 + (N_BEFORE[m] + c) % 2


def phase_mla_heads(nc, a, g):
    ps = g.ps
    with ExitStack() as st:
        def sb(name, shape, dt=F32):
            return st.enter_context(nc.sbuf_tensor(name, shape, dt))

        def sem(name):
            return st.enter_context(nc.semaphore(name))

        w_raw = sb("b_w_raw", [P, HWC])
        w_hi, w_lo = sb("b_w_hi", [P, 2, HWC], R32), sb("b_w_lo", [P, 2, HWC], R32)
        kh, kl = sb("b_kh", [P, 2, SEQ], R32), sb("b_kl", [P, 2, SEQ], R32)
        vh, vl = sb("b_vh", [P, 2, SEQ], R32), sb("b_vl", [P, 2, SEQ], R32)
        qh, ql = sb("b_qh", [P, 2, TOK], R32), sb("b_ql", [P, 2, TOK], R32)
        qr = sb("b_qr", [P, 2, TOK], R32)
        rot = sb("b_rot", [ROPE, 3, CH])
        gate = sb("b_gate", [P, 2, SEQ])
        prob = sb("b_prob", [P, 2, SEQ])
        pth, ptl = sb("b_pth", [P, NT * 2 * P], R32), sb("b_ptl", [P, NT * 2 * P], R32)
        ov, oh, ol = sb("b_ov", [P, 2, 2 * P]), sb("b_oh", [P, 2, 2 * P], R32), sb("b_ol", [P, 2, 2 * P], R32)
        stat = sb("b_stat", [P, 2, 4])
        mask = sb("b_mask", [P, P])
        maskr = sb("b_maskr", [P, P], R32)
        mask_in, mask_ok = sem("b_mask_in"), sem("b_mask_ok")
        w_in, w_rounded, w_split = sem("b_w_in"), sem("b_w_rounded"), sem("b_w_split")
        gate_in = [sem(f"b_gate_in{u}") for u in range(2)]
        pj_done, pj_hi, pj_ready, pj_mul, pj_rot = (sem("b_pj_done"), sem("b_pj_hi"), sem("b_pj_ready"),
                                                    sem("b_pj_mul"), sem("b_pj_rot"))
        kept = sem("b_kept")
        scored, maxed, exped, inverted, normed = (sem("b_scored"), sem("b_maxed"), sem("b_exped"),
                                                  sem("b_inverted"), sem("b_normed"))
        turned, pt_hi, pt_lo = sem("b_turned"), sem("b_pt_hi"), sem("b_pt_lo")
        mixed, gated, o_hi, o_lo = sem("b_mixed"), sem("b_gated"), sem("b_o_hi"), sem("b_o_lo")
        o_out = g.o_out
        block = st.enter_context(nc.Block())

        def turn_chunks(what, m):
            return range(0, min(2, m + 1)) if what == "turn" else range(2, m + 1)

        def head_steps(attend, project):
            attend("score", 0)
            project(0)
            attend("score", 1)
            project(1)
            for m in range(GRP):
                attend("turn", m)
                if m < GRP - 1:
                    attend("score", 2 * m + 2)
                    attend("turn_rest", m)
                    project(2 * m + 2)
                    attend("score", 2 * m + 3)
                    attend("mix", m)
                    project(2 * m + 3)
                else:
                    project(8)
                    attend("turn_rest", m)
                    project(9)
                    attend("mix", m)

        @block.sync
        def _(sp):
            nc.sync.dma_start(mask[:], a["mask"]).then_inc(mask_in, 16)

            def load(h):
                if due(h):
                    sp.wait_ge(w_split, h)
                nc.sync.dma_start(w_raw[:], a["head_w"][ds(h, 1)].rearrange("a p c -> (a p) c")).then_inc(w_in, 16)

            def load_gate(h, u):
                if due(GRP * (h - 1)):
                    sp.wait_ge(gated, GRP * (h - 1))
                nc.sync.dma_start(gate[:, u, :], g.gate_dram[ds(h, 1)].rearrange("a p n -> (a p) n")).then_inc(gate_in[u], 16)

            load(0)
            load(1)
            def body(i):
                for u in range(2):
                    load_gate(2 * i + u, u)
                    load(2 * i + u + 2)
            pairs(sp, H // 2 - 1, body)
            load_gate(H - 2, 0)
            load(H)
            load_gate(H - 1, 1)

        @block.gpsimd
        def _(pool):
            def split(h, u):
                if due(N_PJ * (h - 1)):
                    pool.wait_ge(pj_done, N_PJ * (h - 1))
                pool.wait_ge(w_in, 16 * (h + 1))
                nc.gpsimd.tensor_tensor(w_hi[:, u, :], w_raw[:], g.ones[:, 0:1].to_broadcast([P, HWC]),
                                        ALU.mult).then_inc(w_rounded, 1)
                pool.wait_ge(w_rounded, h + 1)
                nc.gpsimd.tensor_tensor(w_lo[:, u, :], w_raw[:], w_hi[:, u, :].bitcast(F32),
                                        ALU.subtract).then_inc(w_split, 1)

            def cut_output(h, m):
                n, v = GRP * h + m, m % 2
                pool.wait_ge(gated, n + 1)
                if due(32 * (2 * h + m // 2)):
                    pool.wait_ge(o_out[v], 32 * (2 * h + m // 2))
                nc.gpsimd.tensor_tensor(oh[:, v, :], ov[:, v, :], g.ones[:, 0:1].to_broadcast([P, 2 * P]),
                                        ALU.mult).then_inc(o_hi, 1)
                pool.wait_ge(o_hi, n + 1)
                nc.gpsimd.tensor_tensor(ol[:, v, :], ov[:, v, :], oh[:, v, :].bitcast(F32),
                                        ALU.subtract).then_inc(o_lo, 1)
                pool.wait_ge(o_lo, n + 1)
                nc.gpsimd.dma_start(g.oh_dram[ds(h, 1), :, m * 2 * P:(m + 1) * 2 * P].rearrange("a p n -> (a p) n"),
                                    oh[:, v, :].bitcast(F32)).then_inc(o_out[v], 16)
                nc.gpsimd.dma_start(g.ol_dram[ds(h, 1), :, m * 2 * P:(m + 1) * 2 * P].rearrange("a p n -> (a p) n"),
                                    ol[:, v, :].bitcast(F32)).then_inc(o_out[v], 16)

            split(0, 0)
            split(1, 1)
            def head(h, u):
                split(h + 2, u)
                for m in range(GRP):
                    cut_output(h, m)
            pairs(pool, H // 2 - 1, lambda i: [head(2 * i + u, u) for u in range(2)])
            head(H - 2, 0)
            for m in range(GRP):
                cut_output(H - 1, m)
            for v in range(2):
                pool.wait_ge(o_out[v], 32 * 2 * H)

        @block.scalar
        def _(act):
            act.wait_ge(mask_in, 16)
            nc.scalar.activation(maskr[:], mask[:], ACT.Copy).then_inc(mask_ok, 1)

            def project(h, u, j):
                what, c = PJ[j]
                n = N_PJ * h + j
                cols = slice(c * CH, (c + 1) * CH)
                if what == "qn":
                    act.wait_ge(pj_done, n + 1)
                    if c == 2:
                        nc.scalar.activation(g.qs_nope[:, ds(h, 1), :].rearrange("p a n -> p (a n)"),
                                             ps[:, 7, CH - DEC:CH], ACT.Copy, scale=MLA_SCALE).then_inc(kept, 1)
                    nc.scalar.activation(qh[:, u, cols], ps[:, 7, 0:CH], ACT.Copy, scale=MLA_SCALE).then_inc(pj_hi, 1)
                elif what == "qr":
                    act.wait_ge(pj_rot, 3 * h + c + 1)
                    nc.scalar.activation(qr[0:ROPE, u, cols], rot[:, 2, :], ACT.Copy, scale=MLA_SCALE).then_inc(pj_hi, 1)
                    if c == 2:
                        nc.scalar.activation(g.qs_rope[:, ds(h, 1), :].rearrange("p a n -> p (a n)"),
                                             rot[:, 2, CH - DEC:CH], ACT.Copy, scale=MLA_SCALE).then_inc(kept, 1)
                else:
                    act.wait_ge(pj_done, n + 1)
                    dst = kh if what == "k" else vh
                    nc.scalar.activation(dst[:, u, c * 512:(c + 1) * 512], ps[:, 7, :], ACT.Copy).then_inc(pj_hi, 1)

            def attend(h, u, what, m):
                if what == "score":
                    n, r, keys = Q_TILES * h + m, m % 2, (m + 1) * P
                    act.wait_ge(maxed, n + 1)
                    if due(N_PT * h + N_BEFORE[m // 2] if m > 1 else N_PT * h):
                        act.wait_ge(turned, N_PT * h + N_BEFORE[m // 2] if m > 1 else N_PT * h)
                    nc.scalar.activation(prob[:, r, 0:keys],
                                         ps[:, 2 * r:2 * r + 2, :].rearrange("p b n -> p (b n)")[:, 0:keys],
                                         ACT.Exp, bias=stat[:, r, 0:1], accum_out=stat[:, r, 1:2]).then_inc(exped, 1)
                elif what in ("turn", "turn_rest"):
                    if what == "turn":
                        if due(GRP * h + m):
                            act.wait_ge(mixed, GRP * h + m)
                    for c in turn_chunks(what, m):
                        cols, n = (512 if c < m else 384), N_PT * h + N_BEFORE[m] + c
                        act.wait_ge(turned, n + 1)
                        nc.scalar.activation(pth[:, c * 512:c * 512 + cols], ps[:, pt_bank(m, c), 0:cols], ACT.Copy).then_inc(pt_hi, 1)

            for j in range(N_PJ):
                project(0, 0, j)
            def body(i):
                for u in range(2):
                    h = 2 * i + u
                    head_steps(lambda what, m: attend(h, u, what, m), lambda j: project(h + 1, 1 - u, j))
            pairs(act, H // 2, body)

        @block.vector
        def _(dve):
            def project(h, u, j):
                what, c = PJ[j]
                n = N_PJ * h + j
                cols = slice(c * CH, (c + 1) * CH)
                if what == "qn":
                    dve.wait_ge(pj_hi, n + 1)
                    nc.vector.scalar_tensor_tensor(out=ql[:, u, cols], in0=ps[:, 7, 0:CH], scalar=MLA_SCALE,
                                                   in1=qh[:, u, cols].bitcast(F32), op0=ALU.mult,
                                                   op1=ALU.subtract).then_inc(pj_ready, 1)
                elif what == "qr":
                    dve.wait_ge(pj_done, n + 1)
                    if due(2 * h):
                        dve.wait_ge(kept, 2 * h)
                    nc.vector.tensor_tensor(rot[:, 0, :], ps[0:ROPE, 7, 0:CH], g.cs[0:ROPE, cols], ALU.mult).then_inc(pj_mul, 1)
                    nc.vector.tensor_tensor(rot[:, 1, :], ps[ROPE:P, 7, 0:CH], g.cs[ROPE:P, cols], ALU.mult).then_inc(pj_mul, 1)
                    dve.wait_ge(pj_mul, 2 * (3 * h + c + 1))
                    nc.vector.tensor_tensor(rot[:, 2, :], rot[:, 0, :], rot[:, 1, :], ALU.add).then_inc(pj_rot, 1)
                    dve.wait_ge(pj_hi, n + 1)
                    nc.vector.scalar_tensor_tensor(out=qr[ROPE:P, u, cols], in0=rot[:, 2, :], scalar=MLA_SCALE,
                                                   in1=qr[0:ROPE, u, cols].bitcast(F32), op0=ALU.mult,
                                                   op1=ALU.subtract).then_inc(pj_ready, 1)
                else:
                    hi, lo = (kh, kl) if what == "k" else (vh, vl)
                    dve.wait_ge(pj_hi, n + 1)
                    nc.vector.tensor_tensor(lo[:, u, c * 512:(c + 1) * 512], ps[:, 7, :],
                                            hi[:, u, c * 512:(c + 1) * 512].bitcast(F32), ALU.subtract).then_inc(pj_ready, 1)

            def norm(h, m):
                n, r, keys = Q_TILES * h + m, m % 2, (m + 1) * P
                dve.wait_ge(exped, n + 1)
                nc.vector.reciprocal(stat[:, r, 2:3], stat[:, r, 1:2]).then_inc(inverted, 1)
                dve.wait_ge(inverted, n + 1)
                nc.vector.tensor_scalar(prob[:, r, 0:keys], prob[:, r, 0:keys], stat[:, r, 2:3], None,
                                        ALU.mult).then_inc(normed, 1)

            def attend(i, u, what, m):
                h = 2 * i + u
                if what == "score":
                    n, r, keys = Q_TILES * h + m, m % 2, (m + 1) * P
                    if r == 1:
                        norm(h, m - 1)
                    dve.wait_ge(scored, n + 1)
                    nc.vector.tensor_reduce(stat[:, r, 0:1],
                                            ps[:, 2 * r:2 * r + 2, :].rearrange("p b n -> p (b n)")[:, 0:keys],
                                            AX.X, ALU.max, negate=True).then_inc(maxed, 1)
                    if r == 1:
                        norm(h, m)
                elif what in ("turn", "turn_rest"):
                    for c in turn_chunks(what, m):
                        cols, n = (512 if c < m else 384), N_PT * h + N_BEFORE[m] + c
                        dve.wait_ge(pt_hi, n + 1)
                        nc.vector.tensor_tensor(ptl[:, c * 512:c * 512 + cols], ps[:, pt_bank(m, c), 0:cols],
                                                pth[:, c * 512:c * 512 + cols].bitcast(F32),
                                                ALU.subtract).then_inc(pt_lo, 1)
                else:
                    dve.wait_ge(mixed, GRP * h + m + 1)
                    if m == 0:
                        dve.wait_ge(gate_in[u], 16 * (i + 1))
                    if due(GRP * h + m - 1):
                        dve.wait_ge(o_lo, GRP * h + m - 1)
                    nc.vector.tensor_tensor(ov[:, m % 2, :], ps[:, 6, 0:2 * P], gate[:, u, m * 2 * P:(m + 1) * 2 * P],
                                            ALU.mult).then_inc(gated, 1)

            for j in range(N_PJ):
                project(0, 0, j)
            def body(i):
                for u in range(2):
                    h = 2 * i + u
                    head_steps(lambda what, m: attend(i, u, what, m), lambda j: project(h + 1, 1 - u, j))
            pairs(dve, H // 2, body)

        @block.tensor
        def _(pe):
            def project(h, u, j):
                what, c = PJ[j]
                n = N_PJ * h + j
                if j == 0:
                    pe.wait_ge(w_split, h + 1)
                if due(n):
                    pe.wait_ge(pj_ready, n)
                if what in ("qn", "qr"):
                    for k in range(4):
                        o = k * 256 + (P if what == "qr" else 0)
                        for x, (wt, xt) in enumerate(((w_hi, g.cqh), (w_hi, g.cql), (w_lo, g.cqh))):
                            mm = nc.tensor.matmul(ps[:, 7, 0:CH], wt[:, u, o:o + P], xt[:, k, c * CH:(c + 1) * CH],
                                                  start=k == 0 and x == 0, stop=k == 3 and x == 2)
                elif what == "k":
                    for k in range(2):
                        o = QW + k * P
                        for x, (wt, xt) in enumerate(((w_hi, g.ckvh), (w_hi, g.ckvl), (w_lo, g.ckvh))):
                            mm = nc.tensor.matmul(ps[:, 7, :], wt[:, u, o:o + P], xt[:, k, c * 512:(c + 1) * 512],
                                                  start=k == 0 and x == 0, stop=k == 1 and x == 2)
                else:
                    for t in range(4):
                        for k in range(2):
                            o = QW + 2 * P + k * P
                            cols = slice((4 * c + t) * P, (4 * c + t + 1) * P)
                            for x, (xt, wt) in enumerate(((g.ckvh, w_hi), (g.ckvl, w_hi), (g.ckvh, w_lo))):
                                mm = nc.tensor.matmul(ps[:, 7, t * P:(t + 1) * P], xt[:, k, cols], wt[:, u, o:o + P],
                                                      start=k == 0 and x == 0, stop=k == 1 and x == 2)
                mm.then_inc(pj_done, 1)

            def attend(h, u, what, m):
                if what == "score":
                    n, r, q = Q_TILES * h + m, m % 2, slice(m * P, (m + 1) * P)
                    if m == 0:
                        pe.wait_ge(pj_ready, N_PJ * (h + 1) - 2)
                    if due(n - 1):
                        pe.wait_ge(exped, n - 1)
                    for b in range((m * P) // 512 + 1):
                        keys = slice(b * 512, min((m + 1) * P, (b + 1) * 512))
                        own = b == (m * P) // 512
                        out = ps[:, 2 * r + b, 0:keys.stop - keys.start]
                        nc.tensor.matmul(out, qh[:, u, q], kh[:, u, keys], start=True, stop=False)
                        nc.tensor.matmul(out, qh[:, u, q], kl[:, u, keys], start=False, stop=False)
                        nc.tensor.matmul(out, ql[:, u, q], kh[:, u, keys], start=False, stop=False)
                        nc.tensor.matmul(out, qr[:, u, q], g.krh[:, keys], start=False, stop=False)
                        mm = nc.tensor.matmul(out, qr[0:ROPE, u, q], g.krl[:, keys], start=False, stop=not own)
                        if own:
                            mm = nc.tensor.matmul(ps[:, 2 * r + b, (m % 4) * P:(m % 4 + 1) * P], g.identr[:], maskr[:],
                                                  start=False, stop=True)
                    mm.then_inc(scored, 1)
                elif what in ("turn", "turn_rest"):
                    if what == "turn":
                        pe.wait_ge(normed, Q_TILES * h + 2 * m + 2)
                    for c in turn_chunks(what, m):
                        n, bank = N_PT * h + N_BEFORE[m] + c, pt_bank(m, c)
                        if due(n - 1):
                            pe.wait_ge(pt_lo, n - 1)
                        for b in range(2):
                            for q in range(2):
                                if c == m and b == 1 and q == 0:
                                    continue
                                col = b * 256 + q * P - (P if c == m and b == 1 else 0)
                                mm = nc.tensor.transpose(ps[:, bank, col:col + P],
                                                         prob[:, q, (2 * c + b) * P:(2 * c + b + 1) * P], g.ident[:])
                        mm.then_inc(turned, 1)
                else:
                    pe.wait_ge(pt_lo, N_PT * h + N_BEFORE[m] + m + 1)
                    if due(GRP * h + m):
                        pe.wait_ge(gated, GRP * h + m)
                    if m == 0:
                        pe.wait_ge(pj_ready, N_PJ * (h + 1))
                    for k in range(2 * m + 2):
                        wide = 2 * P if k < 2 * m + 1 else P
                        col, v = k * 2 * P, slice(k * P, (k + 1) * P)
                        for x, (vt, pt) in enumerate(((vh, pth), (vh, ptl), (vl, pth))):
                            mm = nc.tensor.matmul(ps[:, 6, 2 * P - wide:2 * P], vt[:, u, v], pt[:, col:col + wide],
                                                  start=k == 0 and x == 0, stop=k == 2 * m + 1 and x == 2)
                    mm.then_inc(mixed, 1)

            pe.wait_ge(mask_ok, 1)
            for j in range(N_PJ):
                project(0, 0, j)
            def body(i):
                for u in range(2):
                    h = 2 * i + u
                    head_steps(lambda what, m: attend(h, u, what, m), lambda j: project(h + 1, 1 - u, j))
            pairs(pe, H // 2, body)




SLOTS = 4
SELF = (NPG + 1) * H


def phase_mla_samples(nc, a, g):
    ps = g.ps
    SW = PAST + 1
    with ExitStack() as st:
        def sb(name, shape, dt=F32):
            return st.enter_context(nc.sbuf_tensor(name, shape, dt))

        def sem(name):
            return st.enter_context(nc.semaphore(name))

        xo_l = g.xo_l
        pages = sb("c_pages", [P, SLOTS, NPG, PGW])
        table = sb("c_table", [1, DEC * NPG], I32)
        turned = sb("c_turned", [P, 2, 3, 512])
        prob = sb("c_prob", [48, SW + 3])
        pt = sb("c_pt", [P, (NPG + 1) * H])
        wk = sb("c_wk", [P, H, KVL])
        q_lat = sb("c_q_lat", [P, 2, DEC, H])
        q_rot = sb("c_q_rot", [ROPE, DEC, H])
        q_b, k_b = sb("c_q_b", [P, 2, 3, H]), sb("c_k_b", [P, 2, 3])
        o_rows = sb("c_o_rows", [48, DEC // 2, KVL])
        o_lat = sb("c_o_lat", [P, DEC // 2, 2, 3, H])
        o_s = sb("c_o_s", [P, H, DEC])
        stat = sb("c_stat", [48, 4])
        new_row = sb("c_new_row", [1, SLOTS, KVL])
        table_in, xo_in = sem("c_table_in"), g.xo_in
        page_in = [sem(f"c_page_in{s}") for s in range(SLOTS)]
        wk_in = sem("c_wk_in")
        cleared, rows_turned, lat_kept = sem("c_cleared"), sem("c_rows_turned"), sem("c_lat_kept")
        q_made, q_kept = sem("c_q_made"), sem("c_q_kept")
        b_copied = sem("c_b_copied")
        t_done, t_lat, t_rot = sem("c_t_done"), sem("c_t_lat"), sem("c_t_rot")
        s_done, s_read = sem("c_s_done"), sem("c_s_read")
        maxed, exped, inverted = sem("c_maxed"), sem("c_exped"), sem("c_inverted")
        p_turned, p_copied, mixed, o_kept, tail_begun = (sem("c_p_turned"), sem("c_p_copied"), sem("c_mixed"),
                                                       sem("c_o_kept"), sem("c_tail_begun"))
        out_made, out_gated, out_hi, out_lo = sem("c_out_made"), sem("c_out_gated"), sem("c_out_hi"), sem("c_out_lo")
        block = st.enter_context(nc.Block())

        def order(eng, lead, tail):
            def body(j):
                lead(j, SLOTS * j, 0)
                for s in range(1, SLOTS):
                    lead(j, SLOTS * j + s, s)
                    tail(j, SLOTS * j + s - 1, s - 1)
                tail(j, SLOTS * j + SLOTS - 1, SLOTS - 1)
            pairs(eng, DEC // SLOTS, body)

        @block.sync
        def _(sp):
            nc.sync.dma_start(table[:], a["page_table"].rearrange("(o b) n -> o (b n)", o=1)).then_inc(table_in, 16)
            nc.sync.dma_start(wk[:], a["w_uk_turned"].rearrange("h p k -> p h k")).then_inc(wk_in, 16)
            sp.wait_ge(table_in, 16)

            def load_pages(b, s):
                if due(b - SLOTS + 1):
                    sp.wait_ge(mixed, b - SLOTS + 1)
                nc.sync.dma_start(new_row[:, s, :], a["new_ckv_sample"][0, ds(b, 1), 0, :]).then_inc(page_in[s], 16)
                for n in range(NPG):
                    page = nc.sync.value_load(table[0:1, ds(b * NPG + n, 1)], min_val=0,
                                              max_val=a["cache_ckv"].shape[1] - 1)
                    nc.sync.dma_start(pages[:, s, n, 0:KVL], a["cache_ckv"][0, ds(page, 1)].rearrange("a p c -> (a p) c")
                                      ).then_inc(page_in[s], 16)
            pairs(sp, DEC // SLOTS, lambda j: [load_pages(SLOTS * j + s, s) for s in range(SLOTS)])
            sp.wait_ge(q_made, 1)
            nc.sync.dma_start(wk[:], a["w_uv_heads"].rearrange("h p k -> p h k")).then_inc(wk_in, 16)

        @block.gpsimd
        def _(pool):
            nc.gpsimd.memset(o_rows[:], 0.0).then_inc(cleared, 1)
            pool.wait_ge(table_in, 16)

            def load_keys(b, s):
                if due(b - SLOTS + 1):
                    pool.wait_ge(mixed, b - SLOTS + 1)
                for n in range(NPG):
                    page = nc.gpsimd.value_load(table[0:1, ds(b * NPG + n, 1)], min_val=0,
                                                max_val=a["cache_kpe"].shape[1] - 1)
                    nc.gpsimd.dma_start(pages[:, s, n, KVL:PGW], a["cache_kpe"][0, ds(page, 1)].rearrange("a p c -> (a p) c")
                                        ).then_inc(g.key_in[s], 16)

            def load_round(j):
                for s in range(SLOTS):
                    load_keys(SLOTS * j + s, s)
            load_round(0)
            for h in range(H):
                nc.gpsimd.dma_start(g.xo_h[:, h, 0:SEQ].bitcast(F32), g.oh_dram[h]).then_inc(xo_in, 16)
            with pool.Fori(1, DEC // SLOTS) as j:
                load_round(j)
            for h in range(H):
                pool.wait_ge(mixed, DEC - SLOTS + 1 + ((h + 1) * TOK - 1) // (NPG * PGW))
                nc.gpsimd.dma_start(xo_l[:, h, 0:SEQ].bitcast(F32), g.ol_dram[h]).then_inc(xo_in, 16)
            pool.wait_ge(xo_in, 16 * 2 * H)

        @block.scalar
        def _(act):
            act.wait_ge(q_made, 1)
            for c in range(2):
                nc.scalar.activation(q_lat[:, c].rearrange("p b h -> p h b"),
                                     ps[:, 0, c * P:(c + 1) * P].rearrange("p (h b) -> p h b", b=DEC),
                                     ACT.Copy).then_inc(q_kept, 1)
            nc.scalar.activation(q_rot[:].rearrange("p b h -> p h b"), g.qs_rope[:, 0:H, :], ACT.Copy).then_inc(q_kept, 1)
            act.wait_ge(q_kept, 3)

            def lead(j, b, s):
                u = s % 2
                if due(5 * (b - 1)):
                    act.wait_ge(s_done, 5 * (b - 1))
                nc.scalar.activation(q_b[:, u, 0:2, :], q_lat[:, :, ds(b, 1), :].rearrange("p c a h -> p c (a h)"),
                                     ACT.Copy).then_inc(b_copied, 1)
                nc.scalar.activation(q_b[0:ROPE, u, 2, :], q_rot[:, ds(b, 1), :].rearrange("p a h -> p (a h)"),
                                     ACT.Copy).then_inc(b_copied, 1)
                nc.scalar.activation(k_b[:, u, 0:2], g.ckv_s[:, 0:2, ds(b, 1)].rearrange("p c a -> p (c a)"),
                                     ACT.Copy).then_inc(b_copied, 1)
                nc.scalar.activation(k_b[0:ROPE, u, 2:3], g.ckv_s[0:ROPE, 2, ds(b, 1)], ACT.Copy).then_inc(b_copied, 1)
                for c in range(4):
                    n, v = 4 * b + c, c % 2
                    act.wait_ge(t_done, n + 1)
                    if due(5 * b + c - 1 if c > 1 else 5 * b - 3 + c):
                        act.wait_ge(s_done, 5 * b + c - 1 if c > 1 else 5 * b - 3 + c)
                    nc.scalar.activation(turned[:, v, 0:2, :], ps[:, 3 * v:3 * v + 2, :], ACT.Copy).then_inc(t_lat, 1)
                    if c == 1 and s > 0:
                        softmax(b - 1, 1 - u)

            def softmax(b, u):
                r = slice(32 * u, 32 * u + H)
                act.wait_ge(maxed, b + 1)
                nc.scalar.activation(prob[r, 0:SW], prob[r, 0:SW], ACT.Exp, bias=stat[r, 0:1],
                                     accum_out=stat[r, 1:2]).then_inc(exped, 1)

            def tail(j, b, s):
                r = slice(32 * (s % 2), 32 * (s % 2) + H)
                if s == SLOTS - 1:
                    softmax(b, s % 2)
                act.wait_ge(p_turned, b + 1)
                nc.scalar.activation(pt[:, 0:NPG * H], ps[:, 7, 0:NPG * H], ACT.Copy).then_inc(p_copied, 1)
                nc.scalar.activation(pt[0:1, NPG * H:], ps[0:1, 7, NPG * H:(NPG + 1) * H], ACT.Copy).then_inc(p_copied, 1)
                act.wait_ge(cleared, 1)
                act.wait_ge(inverted, b + 1)
                act.wait_ge(mixed, b + 1)
                nc.scalar.activation(o_rows[r, ds(SLOTS // 2 * j + s // 2, 1), :].rearrange("p a k -> p (a k)"),
                                     ps[r, 7, KVL:2 * KVL], ACT.Copy, scale=stat[r, 2:3]).then_inc(o_kept, 1)
            order(act, lead, tail)
            act.wait_ge(rows_turned, 1)
            nc.scalar.activation(o_lat[:].rearrange("p i c v h -> p (i c v h)"), ps[:, 1, 0:DEC * 48],
                                 ACT.Copy).then_inc(lat_kept, 1)
            act.wait_ge(out_gated, 1)
            nc.scalar.activation(g.xo_h[:, :, SEQ:TOK], o_s[:], ACT.Copy).then_inc(out_hi, 1)

        @block.vector
        def _(dve):
            def lead(j, b, s):
                u = s % 2
                for c in range(4):
                    n, v = 4 * b + c, c % 2
                    dve.wait_ge(t_done, n + 1)
                    if due(5 * b + c - 1 if c > 1 else 5 * b - 3 + c):
                        dve.wait_ge(s_done, 5 * b + c - 1 if c > 1 else 5 * b - 3 + c)
                    nc.vector.tensor_copy(turned[0:ROPE, v, 2, :], ps[0:ROPE, 3 * v + 2, :]).then_inc(t_rot, 1)
                    if c > 0:
                        scores(b, u, c - 1)
                    if c == 0 and s > 0:
                        greatest(b - 1, 1 - u)
                    if c == 2 and s > 0:
                        invert(b - 1, 1 - u)
                scores(b, u, 3)
                dve.wait_ge(s_done, 5 * b + 5)
                nc.vector.tensor_copy(prob[32 * u:32 * u + H, PAST:SW], ps[32 * u:32 * u + H, 7, SELF:SELF + 1]).then_inc(s_read, 1)

            def scores(b, u, c):
                dve.wait_ge(s_done, 5 * b + c + 1)
                if c == 0:
                    if due(b - 1):
                        dve.wait_ge(p_turned, b - 1)
                nc.vector.tensor_copy(prob[32 * u:32 * u + H, c * 512:(c + 1) * 512],
                                      ps[32 * u:32 * u + H, 6, :]).then_inc(s_read, 1)

            def greatest(b, u):
                r = slice(32 * u, 32 * u + H)
                dve.wait_ge(s_read, 5 * (b + 1))
                if due(b - 1):
                    dve.wait_ge(exped, b - 1)
                nc.vector.tensor_reduce(stat[r, 0:1], prob[r, 0:SW], AX.X, ALU.max, negate=True).then_inc(maxed, 1)

            def invert(b, u):
                r = slice(32 * u, 32 * u + H)
                dve.wait_ge(exped, b + 1)
                if due(b - 1):
                    dve.wait_ge(o_kept, b - 1)
                nc.vector.reciprocal(stat[r, 2:3], stat[r, 1:2]).then_inc(inverted, 1)

            def tail(j, b, s):
                if s == SLOTS - 1:
                    greatest(b, s % 2)
                    invert(b, s % 2)
            order(dve, lead, tail)
            dve.wait_ge(out_made, 1)
            nc.vector.tensor_tensor(o_s[:], ps[:, 0, 0:P].rearrange("p (h b) -> p h b", b=DEC), g.gate_s[:],
                                    ALU.mult).then_inc(out_gated, 1)
            dve.wait_ge(out_hi, 1)
            dve.wait_ge(mixed, DEC)
            nc.vector.tensor_tensor(xo_l[:, :, SEQ:TOK], o_s[:], g.xo_h[:, :, SEQ:TOK].bitcast(F32),
                                    ALU.subtract).then_inc(out_lo, 1)

        @block.tensor
        def _(pe):
            pe.wait_ge(wk_in, 16)
            for h in range(H):
                for c in range(2):
                    mm = nc.tensor.matmul(ps[:, 0, c * P + h * DEC:c * P + (h + 1) * DEC], wk[:, h, c * P:(c + 1) * P],
                                          g.qs_nope[:, h, :], start=True, stop=True)
            mm.then_inc(q_made, 1)
            pe.wait_ge(q_kept, 3)

            def lead(j, b, s):
                u = s % 2
                r = slice(32 * u, 32 * u + H)

                def turn(c):
                    n, v = 4 * b + c, c % 2
                    if due(n - 1):
                        pe.wait_ge(t_lat, n - 1)
                    if due(n - 1):
                        pe.wait_ge(t_rot, n - 1)
                    if c == 0:
                        pe.wait_ge(page_in[s], 16 * (NPG + 1) * (j + 1))
                        pe.wait_ge(g.key_in[s], 16 * NPG * (j + 1))
                    for k in range(4):
                        for f in range(3):
                            width = P if f < 2 else ROPE
                            mm = nc.tensor.transpose(ps[0:width, 3 * v + f, k * P:(k + 1) * P],
                                                     pages[:, s, 4 * c + k, f * P:f * P + width], g.ident[:])
                    mm.then_inc(t_done, 1)

                def score(c):
                    n, v = 4 * b + c, c % 2
                    pe.wait_ge(t_lat, n + 1)
                    pe.wait_ge(t_rot, n + 1)
                    if due(5 * b + c):
                        pe.wait_ge(s_read, 5 * b + c)
                    if c == 0:
                        pe.wait_ge(b_copied, 4 * (b + 1))
                    nc.tensor.matmul(ps[r, 6, :], q_b[:, u, 0, :], turned[:, v, 0, :], start=True, stop=False)
                    nc.tensor.matmul(ps[r, 6, :], q_b[:, u, 1, :], turned[:, v, 1, :], start=False, stop=False)
                    nc.tensor.matmul(ps[r, 6, :], q_b[0:ROPE, u, 2, :], turned[0:ROPE, v, 2, :], start=False,
                                     stop=True).then_inc(s_done, 1)
                turn(0)
                turn(1)
                score(0)
                turn(2)
                score(1)
                turn(3)
                score(2)
                score(3)
                if due(b - 1 if s else b):
                    pe.wait_ge(o_kept, b - 1 if s else b)
                nc.tensor.matmul(ps[r, 7, SELF:SELF + 1], q_b[:, u, 0, :], k_b[:, u, 0:1], start=True, stop=False)
                nc.tensor.matmul(ps[r, 7, SELF:SELF + 1], q_b[:, u, 1, :], k_b[:, u, 1:2], start=False, stop=False)
                nc.tensor.matmul(ps[r, 7, SELF:SELF + 1], q_b[0:ROPE, u, 2, :], k_b[0:ROPE, u, 2:3], start=False,
                                 stop=True).then_inc(s_done, 1)

            def tail(j, b, s):
                r = slice(32 * (s % 2), 32 * (s % 2) + H)
                pe.wait_ge(exped, b + 1)
                if due(b):
                    pe.wait_ge(o_kept, b)
                pe.wait_ge(s_read, 5 * (b + 2) if s < SLOTS - 1 else 5 * (b + 1))
                pe.sem_inc(tail_begun, 1)
                for n in range(NPG):
                    nc.tensor.transpose(ps[:, 7, n * H:(n + 1) * H], prob[r, n * PAGE:(n + 1) * PAGE], g.ident[r, r])
                nc.tensor.transpose(ps[0:1, 7, NPG * H:(NPG + 1) * H], prob[r, PAST:SW], g.ident[r, r]).then_inc(p_turned, 1)
                pe.wait_ge(p_copied, 2 * (b + 1))
                for n in range(NPG):
                    nc.tensor.matmul(ps[r, 7, KVL:2 * KVL], pt[:, n * H:(n + 1) * H], pages[:, s, n, 0:KVL],
                                     start=n == 0, stop=False)
                nc.tensor.matmul(ps[r, 7, KVL:2 * KVL], pt[0:1, NPG * H:], new_row[:, s, :], start=False,
                                 stop=True).then_inc(mixed, 1)
            order(pe, lead, tail)
            pe.wait_ge(o_kept, DEC)
            for i in range(DEC // 2):
                for c in range(2):
                    n = 2 * i + c
                    mm = nc.tensor.transpose(ps[:, 1, n * 48:(n + 1) * 48], o_rows[:, i, c * P:(c + 1) * P], g.ident[0:48, 0:48])
            mm.then_inc(rows_turned, 1)
            pe.wait_ge(lat_kept, 1)
            pe.wait_ge(wk_in, 32)
            for h in range(H):
                for c in range(2):
                    mm = nc.tensor.matmul(ps[:, 0, h * DEC:(h + 1) * DEC], wk[:, h, c * P:(c + 1) * P],
                                          o_lat[:, :, c, 0:3:2, h], start=c == 0, stop=c == 1)
            mm.then_inc(out_made, 1)


def phase_out(nc, a, g, tag, base, xh, xl, halves):
    ps = g.ps
    with ExitStack() as st:
        w = Weights(nc, st, tag)
        read = st.enter_context(nc.semaphore(f"{tag}_read"))
        block = st.enter_context(nc.Block())

        @block.sync
        def _(sp):
            load_weights(nc, sp, w, a["w_tiles"], base, KT * halves)

        @block.gpsimd
        def _(pool):
            split_weights(nc, pool, w, g.ones, KT * halves)

        @block.scalar
        def _(act):
            def body(i):
                for u in range(2):
                    act.wait_ge(w.used, halves * (2 * i + u + 1))
                    nc.scalar.activation(g.mt[:, ds(2 * i + u, 1), :].rearrange("p a (c n) -> p (a c) n", c=3),
                                         psum3(ps, u), ACT.Copy).then_inc(read, 1)
            pairs(act, KT // 2, body)

        @block.tensor
        def _(pe):
            def body(i):
                for u in range(2):
                    j = 2 * i + u
                    if due(j - 1):
                        pe.wait_ge(read, j - 1)
                    for s in range(halves):
                        slot = s if halves == 2 else u
                        pe.wait_ge(w.split, halves * j + s + 1)
                        job_matmuls(nc, w, slot, ps, 3 * u, xh, xl, s * KT, s == 0, s == halves - 1).then_inc(w.used, 1)
            pairs(pe, KT // 2, body)


def phase_norms(nc, a, g, layer):
    ps, tag = g.ps, f"n{layer}"
    more = layer == 0
    with ExitStack() as st:
        def sb(name, shape, dt=F32):
            return st.enter_context(nc.sbuf_tensor(f"{tag}_{name}", shape, dt))

        def sem(name):
            return st.enter_context(nc.semaphore(f"{tag}_{name}"))

        post = sb("post", [P, D])
        res, y, h1 = sb("res", [P, 2, D]), sb("y", [P, 2, D]), sb("h1", [P, 2, D])
        junk = sb("junk", [P, D])
        stat, stat2 = sb("stat", [P, 2, 3]), sb("stat2", [P, 2, 3])
        post_in, negated = sem("post_in"), sem("negated")
        res_in = [sem(f"res_in{u}") for u in range(2)]
        turned, squared, rooted, inverted, normed, summed = (sem("turned"), sem("squared"), sem("rooted"),
                                                             sem("inverted"), sem("normed"), sem("summed"))
        stored = [sem(f"stored{u}") for u in range(2)]
        if more:
            junk2 = sb("junk2", [P, D])
            x_s, x_g = sb("x_s", [P, 2, D]), sb("x_g", [P, 2, D])
            squared2, rooted2, inverted2, scaled, turned2, gained, x_hi, x_lo = (
                sem(n) for n in ("squared2", "rooted2", "inverted2", "scaled", "turned2", "gained", "x_hi", "x_lo"))
        block = st.enter_context(nc.Block())

        def tiles(eng, body):
            def both(i):
                for u in range(2):
                    body(i, u, P)
            pairs(eng, NT // 2, both)
            body(NT // 2, 0, DEC)

        def staggered(eng, first, then):
            def both(i, after):
                then(i, 0, P, lambda: first(i, 1, P))
                then(i, 1, P, lambda: first(i + 1, 0, after))
            first(0, 0, P)
            both(0, P)
            with eng.Fori(1, NT // 2 - 1) as i:
                both(i, P)
            both(NT // 2 - 1, DEC)
            then(NT // 2, 0, DEC, lambda: None)

        @block.sync
        def _(sp):
            nc.sync.dma_start(post[:], a["post_gain"][layer]).then_inc(post_in, 16)
            if more:
                nc.sync.dma_start(g.sinks[:], a["sinks"]).then_inc(post_in, 16)

            def load(i, u, rows):
                t = 2 * i + u
                if due(t - 1):
                    sp.wait_ge(summed, t - 1)
                if rows < P:
                    src = a["x_sample"] if more else g.h1_dram[SEQ:TOK, :]
                else:
                    src = (a["x_prompt"] if more else g.h1_dram)[ds(t * P, P), :]
                nc.sync.dma_start(res[0:rows, u, :], src).then_inc(res_in[u], 16)
            tiles(sp, load)

        if more:
            @block.gpsimd
            def _(pool):
                def body(i, u, rows):
                    t = 2 * i + u
                    pool.wait_ge(x_hi, t + 1)
                    nc.gpsimd.tensor_tensor(g.xl[:, :, ds(t * P, rows)],
                                            x_g[:, u, :].rearrange("p (k n) -> p k n", k=KT)[:, :, 0:rows],
                                            g.xh[:, :, ds(t * P, rows)].bitcast(F32), ALU.subtract).then_inc(x_lo, 1)
                tiles(pool, body)

        @block.scalar
        def _(act):
            def store(i, u, rows):
                t = 2 * i + u
                act.wait_ge(summed, t + 1)
                if more:
                    dst = g.h1_dram[ds(t * P, P), :] if rows == P else g.h1_dram[SEQ:TOK, :]
                else:
                    dst = a["y_prompt"][0, ds(t * P, P), :] if rows == P else a["y_sample"][:, 0, :]
                nc.scalar.dma_start(dst, h1[0:rows, u, :]).then_inc(stored[u], 16)

            def first(i, u, rows):
                t = 2 * i + u
                act.wait_ge(turned, t + 1)
                nc.scalar.activation(junk[0:rows, :].rearrange("p (b n) -> p b n", b=2), ps[0:rows, 2 * u:2 * u + 2, :],
                                     ACT.Square, accum_out=stat[0:rows, u, 0:1]).then_inc(squared, 1)
                act.wait_ge(squared, t + 1)
                if due(t - 1):
                    act.wait_ge(inverted, t - 1)
                nc.scalar.activation(stat[0:rows, u, 1:2], stat[0:rows, u, 0:1], ACT.Sqrt, scale=1.0 / D,
                                     bias=g.eps[0:rows]).then_inc(rooted, 1)

            def then(i, u, rows, ahead):
                t = 2 * i + u
                store(i, u, rows)
                if more:
                    nc.scalar.activation(junk2[0:rows], h1[0:rows, u, :], ACT.Square,
                                         accum_out=stat2[0:rows, u, 0:1]).then_inc(squared2, 1)
                    act.wait_ge(squared2, t + 1)
                    if due(t - 1):
                        act.wait_ge(inverted2, t - 1)
                    nc.scalar.activation(stat2[0:rows, u, 1:2], stat2[0:rows, u, 0:1], ACT.Sqrt, scale=1.0 / D,
                                         bias=g.eps[0:rows]).then_inc(rooted2, 1)
                ahead()
                if more:
                    act.wait_ge(gained, t + 1)
                    nc.scalar.activation(g.xh[:, :, ds(t * P, rows)],
                                         x_g[:, u, :].rearrange("p (k n) -> p k n", k=KT)[:, :, 0:rows],
                                         ACT.Copy).then_inc(x_hi, 1)
            staggered(act, first, then)
            act.wait_ge(stored[0], 16 * 5)
            act.wait_ge(stored[1], 16 * 4)

        @block.vector
        def _(dve):
            dve.wait_ge(post_in, 32 if more else 16)
            if more:
                nc.vector.tensor_scalar(g.nsinks[:], g.sinks[:], -1.0, None, ALU.mult).then_inc(negated, 1)

            def first(i, u, rows):
                t = 2 * i + u
                dve.wait_ge(rooted, t + 1)
                nc.vector.reciprocal(stat[0:rows, u, 2:3], stat[0:rows, u, 1:2]).then_inc(inverted, 1)
                dve.wait_ge(inverted, t + 1)
                nc.vector.scalar_tensor_tensor(out=y[0:rows, u, :].rearrange("p (b n) -> p b n", b=2),
                                               in0=ps[0:rows, 2 * u:2 * u + 2, :], scalar=stat[0:rows, u, 2:3],
                                               in1=post[0:rows].rearrange("p (b n) -> p b n", b=2),
                                               op0=ALU.mult, op1=ALU.mult).then_inc(normed, 1)
                dve.wait_ge(normed, t + 1)
                dve.wait_ge(res_in[u], 16 * (i + 1))
                if due(16 * i):
                    dve.wait_ge(stored[u], 16 * i)
                if more:
                    if due(t - 1):
                        dve.wait_ge(squared2, t - 1)
                nc.vector.tensor_tensor(h1[0:rows, u, :], y[0:rows, u, :], res[0:rows, u, :], ALU.add).then_inc(summed, 1)

            def then(i, u, rows, ahead):
                t = 2 * i + u
                if more:
                    dve.wait_ge(rooted2, t + 1)
                    nc.vector.reciprocal(stat2[0:rows, u, 2:3], stat2[0:rows, u, 1:2]).then_inc(inverted2, 1)
                    dve.wait_ge(inverted2, t + 1)
                    if due(t - 1):
                        dve.wait_ge(turned2, t - 1)
                    nc.vector.tensor_scalar(x_s[0:rows, u, :], h1[0:rows, u, :], stat2[0:rows, u, 2:3], None,
                                            ALU.mult).then_inc(scaled, 1)
                ahead()
                if more:
                    dve.wait_ge(turned2, t + 1)
                    if due(t - 1):
                        dve.wait_ge(x_lo, t - 1)
                    nc.vector.tensor_tensor(x_g[:, u, :].rearrange("p (k n) -> p k n", k=KT)[:, :, 0:rows],
                                            ps[:, 4 + 2 * u:6 + 2 * u, :].rearrange("p b (k n) -> p (b k) n", k=4)[:, :, 0:rows],
                                            g.gains[:, KT:2 * KT].unsqueeze(2).to_broadcast([P, KT, rows]),
                                            ALU.mult).then_inc(gained, 1)
            staggered(dve, first, then)

        @block.tensor
        def _(pe):
            def turn(t):
                rows, u = (P if t < NT else DEC), t % 2
                if due(t - 1):
                    pe.wait_ge(normed, t - 1)
                for k in range(KT):
                    mm = nc.tensor.transpose(ps[0:rows, 2 * u + k // 4, (k % 4) * P:(k % 4 + 1) * P],
                                             g.mt[:, k, t * P:t * P + rows], g.ident[:])
                mm.then_inc(turned, 1)
            turn(0)
            for t in range(NT + 1):
                rows, u = (P if t < NT else DEC), t % 2
                if t < NT:
                    turn(t + 1)
                if more:
                    pe.wait_ge(scaled, t + 1)
                    if due(t - 1):
                        pe.wait_ge(gained, t - 1)
                    for k in range(KT):
                        mm = nc.tensor.transpose(ps[:, 4 + 2 * u + k // 4, (k % 4) * P:(k % 4) * P + rows],
                                                 x_s[0:rows, u, k * P:(k + 1) * P], g.ident[0:rows, 0:rows])
                    mm.then_inc(turned2, 1)


def phase_swa_in(nc, a, g):
    ps = g.ps
    NQ = 8
    with ExitStack() as st:
        def sb(name, shape, dt=F32):
            return st.enter_context(nc.sbuf_tensor(name, shape, dt))

        def sem(name):
            return st.enter_context(nc.semaphore(name))

        w = Weights(nc, st, "f")
        q_h, q_l = sb("f_q_h", [P, 2, TOK], R32), sb("f_q_l", [P, 2, TOK], R32)
        gate = sb("f_gate", [P, 2, TOK])
        hi, read, kept, zeroed = sem("f_hi"), sem("f_read"), sem("f_kept"), sem("f_zeroed")
        q_out = [sem(f"f_q_out{u}") for u in range(2)]
        gate_out = [sem(f"f_gate_out{u}") for u in range(2)]
        block = st.enter_context(nc.Block())
        NKV = 4

        @block.sync
        def _(sp):
            load_weights(nc, sp, w, a["w_tiles"], B_SIN, N_SIN)

        @block.gpsimd
        def _(pool):
            split_weights(nc, pool, w, g.ones, N_SIN)

        @block.scalar
        def _(act):
            def query(i):
                for u in range(2):
                    j = 2 * i + u
                    act.wait_ge(w.used, j + 1)
                    if due(32 * i):
                        act.wait_ge(q_out[u], 32 * i)
                    nc.scalar.activation(g.q_s[:, ds(j, 1), :].rearrange("p a n -> p (a n)"),
                                         ps[:, 3 * u + 2, CH - DEC:CH], ACT.Copy, scale=SWA_SCALE).then_inc(kept, 1)
                    nc.scalar.activation(chunks(q_h[:, u, :]), psum3(ps, u), ACT.Copy, scale=SWA_SCALE).then_inc(hi, 1)
                    act.wait_ge(read, j + 1)
                    nc.scalar.dma_start(g.qh_dram[ds(j, 1)].rearrange("a p n -> (a p) n"), q_h[:, u, 0:SEQ].bitcast(F32)).then_inc(q_out[u], 16)
                    nc.scalar.dma_start(g.ql_dram[ds(j, 1)].rearrange("a p n -> (a p) n"), q_l[:, u, 0:SEQ].bitcast(F32)).then_inc(q_out[u], 16)
            pairs(act, NQ // 2, query)
            for j in range(2):
                u, n = j % 2, NQ + j
                act.wait_ge(w.used, n + 1)
                nc.scalar.activation(chunks(g.kT[:, j, :]), psum3(ps, u), ACT.Copy).then_inc(hi, 1)
                act.wait_ge(hi, n + 1)
                nc.scalar.activation(g.k_h[:, j, P:P + SEQ], g.kT[:, j, 0:SEQ], ACT.Copy).then_inc(kept, 1)
            for j in range(2):
                n = NQ + 2 + j
                act.wait_ge(w.used, n + 1)
                nc.scalar.activation(chunks(g.vT[:, j, :]), psum3(ps, j % 2), ACT.Copy).then_inc(hi, 1)

            def gates(i):
                for u in range(2):
                    j = 2 * i + u
                    act.wait_ge(w.used, NQ + NKV + j + 1)
                    if due(16 * i):
                        act.wait_ge(gate_out[u], 16 * i)
                    nc.scalar.activation(chunks(gate[:, u, :]), psum3(ps, u), ACT.Silu).then_inc(hi, 1)
                    act.wait_ge(hi, NQ + NKV + j + 1)
                    nc.scalar.dma_start(g.sgate_dram[ds(j, 1)].rearrange("a p n -> (a p) n"), gate[:, u, 0:SEQ]).then_inc(gate_out[u], 16)
                    nc.scalar.activation(g.sgate_s[:, ds(j, 1), :].rearrange("p a n -> p (a n)"), gate[:, u, SEQ:TOK],
                                         ACT.Copy).then_inc(kept, 1)
                    act.wait_ge(kept, NQ + 2 + j + 1)
            pairs(act, NQ // 2, gates)
            for u in range(2):
                act.wait_ge(q_out[u], 32 * NQ // 2)
                act.wait_ge(gate_out[u], 16 * NQ // 2)

        @block.vector
        def _(dve):
            nc.vector.memset(g.k_h[:, :, 0:P].bitcast(F32), 0.0).then_inc(zeroed, 1)
            nc.vector.memset(g.k_l[:, :, 0:P].bitcast(F32), 0.0).then_inc(zeroed, 1)

            def query(i):
                for u in range(2):
                    j = 2 * i + u
                    dve.wait_ge(hi, j + 1)
                    nc.vector.scalar_tensor_tensor(out=chunks(q_l[:, u, :]), in0=psum3(ps, u), scalar=SWA_SCALE,
                                                   in1=chunks(q_h[:, u, :]).bitcast(F32), op0=ALU.mult,
                                                   op1=ALU.subtract).then_inc(read, 1)
            pairs(dve, NQ // 2, query)
            for j in range(2):
                dve.wait_ge(kept, NQ + j + 1)
                nc.vector.tensor_tensor(g.k_l[:, j, P:P + SEQ], g.kT[:, j, 0:SEQ], g.k_h[:, j, P:P + SEQ].bitcast(F32),
                                        ALU.subtract).then_inc(read, 1)

        @block.tensor
        def _(pe):
            def job(n, slot, queries):
                pe.wait_ge(w.split, n + 1)
                if queries:
                    if due(n - 1):
                        pe.wait_ge(read, n - 1)
                else:
                    pe.wait_ge(hi, n - 1)
                job_matmuls(nc, w, slot, ps, 3 * slot, g.xh, g.xl, 0, True, True).then_inc(w.used, 1)
            pairs(pe, NQ // 2, lambda i: [job(2 * i + u, u, True) for u in range(2)])
            pe.wait_ge(read, NQ)
            with pe.Fori(NQ // 2, N_SIN // 2) as i:
                for u in range(2):
                    job(2 * i + u, u, False)


def phase_swa_attention(nc, a, g):
    ps = g.ps
    UNITS = [(gp, ab, half) for gp in range(2) for ab in range(2) for half in range(2)]
    NU = len(UNITS)
    R = 4
    with ExitStack() as st:
        def sb(name, shape, dt=F32):
            return st.enter_context(nc.sbuf_tensor(name, shape, dt))

        def sem(name):
            return st.enter_context(nc.semaphore(name))

        bias_h, bias_l = sb("s_bias_h", [P, H, 256], R32), sb("s_bias_l", [P, H, 256], R32)
        neg, negr = sb("s_neg", [P, P]), sb("s_negr", [P, P], R32)
        v_h, v_l = sb("s_v_h", [P, NT + 1, 256], R32), sb("s_v_l", [P, NT + 1, 256], R32)
        q_h, q_l = sb("s_q_h", [P, 2, SEQ], R32), sb("s_q_l", [P, 2, SEQ], R32)
        gate = sb("s_gate", [P, 2, SEQ])
        prob = sb("s_prob", [P, 2, D])
        pth, ptl = sb("s_pth", [P, D], R32), sb("s_ptl", [P, D], R32)
        ov = sb("s_ov", [P, 2, SEQ])
        tok = sb("s_tok", [P, 2, 512])
        stat = sb("s_stat", [P, 2, 4, 4])
        bias_in = [sem(f"s_bias_in{u}") for u in range(2)]
        neg_in, neg_ok = sem("s_neg_in"), sem("s_neg_ok")
        b_hi, b_lo = sem("s_b_hi"), sem("s_b_lo")
        v_turned, v_hi, v_lo, v_zero = sem("s_v_turned"), sem("s_v_hi"), sem("s_v_lo"), sem("s_v_zero")
        tok_turned, tok_copied, tok_out = sem("s_tok_turned"), sem("s_tok_copied"), sem("s_tok_out")
        q_in = [sem(f"s_q_in{u}") for u in range(2)]
        scored, maxed, sunk, exped = sem("s_scored"), sem("s_maxed"), sem("s_sunk"), sem("s_exped")
        summed, inverted, normed = sem("s_summed"), sem("s_inverted"), sem("s_normed")
        turned, pt_hi, pt_lo, mixed, gated = (sem("s_turned"), sem("s_pt_hi"), sem("s_pt_lo"), sem("s_mixed"), sem("s_gated"))
        y_hi, y_lo = sem("s_y_hi"), sem("s_y_lo")
        block = st.enter_context(nc.Block())

        def order(eng, first, then):
            def step(r, last):
                for n in range(NU):
                    m = n + 2
                    if m < NU:
                        ahead = lambda: first(r, m)
                    elif not last:
                        ahead = lambda: first(r + 1, m - NU)
                    else:
                        ahead = lambda: None
                    then(r, n, ahead)
            first(0, 0)
            first(0, 1)
            step(0, False)
            with eng.Fori(1, R - 1) as r:
                step(r, False)
            step(R - 1, True)

        @block.sync
        def _(sp):
            nc.sync.dma_start(neg[:], a["never"]).then_inc(neg_in, 16)
            for c in range(4):
                if due(c - 1):
                    sp.wait_ge(b_lo, c - 1)
                nc.sync.dma_start(prob[:, c % 2, :], a["swa_bias"][:, c * D:(c + 1) * D]).then_inc(bias_in[c % 2], 16)

            def load(r):
                for gp in range(2):
                    qt = gp * R + r
                    if due(NU * (r - 1) + 4 * (gp + 1)):
                        sp.wait_ge(mixed, NU * (r - 1) + 4 * (gp + 1))
                    if due(NU * (r - 1) + 4 * (gp + 1)):
                        sp.wait_ge(gated, NU * (r - 1) + 4 * (gp + 1))
                    for dst, src in ((q_h, g.qh_dram), (q_l, g.ql_dram), (gate, g.sgate_dram)):
                        nc.sync.dma_start(dst[:, gp, :].bitcast(F32), src[ds(qt, 1)].rearrange("a p n -> (a p) n")).then_inc(q_in[gp], 16)
            pairs(sp, R, load)

        @block.gpsimd
        def _(pool):
            def step(r):
                for n, (gp, ab, half) in enumerate(UNITS):
                    unit, v = NU * r + n, n % 2
                    pool.wait_ge(inverted, unit + 1)
                    nc.gpsimd.tensor_tensor(prob[:, v, :].rearrange("p (n k) -> p n k", n=4),
                                            prob[:, v, :].rearrange("p (n k) -> p n k", n=4),
                                            stat[:, v, 3, :].unsqueeze(2).to_broadcast([P, 4, 256]),
                                            ALU.mult).then_inc(normed, 1)
                    if n == 6:
                        cut(r, 0)
                    elif n == 2 and not (isinstance(r, int) and r == 0):
                        cut(r - 1, 1)

            def cut(r, gp):
                pool.wait_ge(y_hi, 2 * r + gp + 1)
                nc.gpsimd.tensor_tensor(g.xl[:, ds(gp * R + r, 1), 0:SEQ].rearrange("p a n -> p (a n)"), ov[:, gp, :],
                                        g.xh[:, ds(gp * R + r, 1), 0:SEQ].rearrange("p a n -> p (a n)").bitcast(F32),
                                        ALU.subtract).then_inc(y_lo, 1)
            pairs(pool, R, step)
            cut(R - 1, 1)

        @block.scalar
        def _(act):
            act.wait_ge(neg_in, 16)
            nc.scalar.activation(negr[:], neg[:], ACT.Copy).then_inc(neg_ok, 1)
            for c in range(4):
                act.wait_ge(bias_in[c % 2], 16 * (c // 2 + 1))
                nc.scalar.activation(bias_h[:, 4 * c:4 * c + 4, :].rearrange("p h k -> p (h k)"), prob[:, c % 2, :],
                                     ACT.Copy).then_inc(b_hi, 1)
            for c in range(4):
                act.wait_ge(v_turned, c + 1)
                nc.scalar.activation(v_h[:, 1 + 2 * c:3 + 2 * c, :], ps[:, c % 2, :].rearrange("p (b n) -> p b n", b=2),
                                     ACT.Copy).then_inc(v_hi, 1)
            for c in range(2):
                act.wait_ge(tok_copied, c + 1)
            nc.scalar.dma_start(a["new_swa_k_prompt"].rearrange("l b t h d -> (l b t) (h d)"), tok[:, 0, 0:256]).then_inc(tok_out, 16)
            nc.scalar.dma_start(a["new_swa_v_prompt"].rearrange("l b t h d -> (l b t) (h d)"), tok[:, 0, 256:512]).then_inc(tok_out, 16)
            nc.scalar.dma_start(g.kvs_dram, tok[0:DEC, 1, :]).then_inc(tok_out, 16)

            def exponents(r, n):
                gp, ab, half = UNITS[n]
                unit, v, hp = NU * r + n, n % 2, (gp * R + r) * 2 + ab
                act.wait_ge(sunk, unit + 1)
                if due(unit - 1):
                    act.wait_ge(turned, unit - 1)
                for k in range(4):
                    ps_k = ps[:, 2 * v + k // 2, (k % 2) * 256:(k % 2 + 1) * 256]
                    nc.scalar.activation(prob[:, v, k * 256:(k + 1) * 256], ps_k, ACT.Exp, bias=stat[:, v, 0, k:k + 1],
                                         accum_out=stat[:, v, 1, k:k + 1])
                nc.scalar.activation(stat[:, v, 2, :], stat[:, v, 0, :], ACT.Exp,
                                     bias=g.sinks[:, ds(hp, 1)]).then_inc(exped, 1)

            def close(r, n, ahead):
                unit = NU * r + n
                act.wait_ge(turned, unit + 1)
                if due(unit):
                    act.wait_ge(mixed, unit)
                nc.scalar.activation(pth[:].rearrange("p (b n) -> p b n", b=2), ps[:, 4:6, :], ACT.Copy).then_inc(pt_hi, 1)
                ahead()
                if n == 0 and not (isinstance(r, int) and r == 0):
                    output_high(r - 1, 1)
                elif n == 4:
                    output_high(r, 0)

            def output_high(r, gp):
                act.wait_ge(gated, NU * r + 4 * (gp + 1))
                nc.scalar.activation(g.xh[:, ds(gp * R + r, 1), 0:SEQ].rearrange("p a n -> p (a n)"), ov[:, gp, :],
                                     ACT.Copy).then_inc(y_hi, 1)
            order(act, exponents, close)
            output_high(R - 1, 1)
            act.wait_ge(tok_out, 48)

        @block.vector
        def _(dve):
            nc.vector.memset(v_h[:, 0, :].bitcast(F32), 0.0).then_inc(v_zero, 1)
            nc.vector.memset(v_l[:, 0, :].bitcast(F32), 0.0).then_inc(v_zero, 1)
            for c in range(4):
                dve.wait_ge(b_hi, c + 1)
                nc.vector.tensor_tensor(bias_l[:, 4 * c:4 * c + 4, :].rearrange("p h k -> p (h k)"), prob[:, c % 2, :],
                                        bias_h[:, 4 * c:4 * c + 4, :].rearrange("p h k -> p (h k)").bitcast(F32),
                                        ALU.subtract).then_inc(b_lo, 1)
            for c in range(4):
                dve.wait_ge(v_hi, c + 1)
                nc.vector.tensor_tensor(v_l[:, 1 + 2 * c:3 + 2 * c, :], ps[:, c % 2, :].rearrange("p (b n) -> p b n", b=2),
                                        v_h[:, 1 + 2 * c:3 + 2 * c, :].bitcast(F32), ALU.subtract).then_inc(v_lo, 1)
            for c, rows in ((0, P), (1, DEC)):
                dve.wait_ge(tok_turned, c + 1)
                nc.vector.tensor_copy(tok[0:rows, c, :], ps[0:rows, 2 + c, :]).then_inc(tok_copied, 1)

            def close(r, n, ahead):
                gp, ab, half = UNITS[n]
                unit, v, b = NU * r + n, n % 2, ab * 64
                dve.wait_ge(pt_hi, unit + 1)
                nc.vector.tensor_tensor(ptl[:].rearrange("p (b n) -> p b n", b=2), ps[:, 4:6, :],
                                        pth[:].rearrange("p (b n) -> p b n", b=2).bitcast(F32), ALU.subtract).then_inc(pt_lo, 1)
                ahead()
                dve.wait_ge(mixed, unit + 1)
                if ab == 0 and half == 0:
                    if due(2 * r + gp - 1):
                        dve.wait_ge(y_lo, 2 * r + gp - 1)
                nc.vector.tensor_tensor(ov[b:b + 64, gp, half * 512:(half + 1) * 512], ps[b:b + 64, 6 + v, :],
                                        gate[b:b + 64, gp, half * 512:(half + 1) * 512], ALU.mult).then_inc(gated, 1)

            def statistics(r, n):
                gp, ab, half = UNITS[n]
                unit, v, hp = NU * r + n, n % 2, (gp * R + r) * 2 + ab
                dve.wait_ge(scored, unit + 1)
                nc.vector.tensor_reduce(stat[:, v, 0, :], ps[:, 2 * v:2 * v + 2, :].rearrange("p b (n k) -> p (b n) k", n=2),
                                        AX.X, ALU.max, negate=True).then_inc(maxed, 1)
                dve.wait_ge(maxed, unit + 1)
                nc.vector.tensor_scalar(stat[:, v, 0, :], stat[:, v, 0, :], g.nsinks[:, ds(hp, 1)], None,
                                        ALU.min).then_inc(sunk, 1)
                dve.wait_ge(exped, unit + 1)
                nc.vector.tensor_tensor(stat[:, v, 1, :], stat[:, v, 1, :], stat[:, v, 2, :], ALU.add).then_inc(summed, 1)
                dve.wait_ge(summed, unit + 1)
                nc.vector.reciprocal(stat[:, v, 3, :], stat[:, v, 1, :]).then_inc(inverted, 1)

            order(dve, statistics, close)

        @block.tensor
        def _(pe):
            for c in range(4):
                if due(c - 1):
                    pe.wait_ge(v_lo, c - 1)
                for b in range(2):
                    for j in range(2):
                        t = 2 * c + b
                        mm = nc.tensor.transpose(ps[:, c % 2, b * 256 + j * P:b * 256 + (j + 1) * P],
                                                 g.vT[:, j, t * P:(t + 1) * P], g.ident[:])
                mm.then_inc(v_turned, 1)
            for c, (lo, rows) in enumerate(((SEQ - P, P), (SEQ, DEC))):
                for j in range(4):
                    src = (g.kT if j < 2 else g.vT)[:, j % 2, lo:lo + rows]
                    mm = nc.tensor.transpose(ps[0:rows, 2 + c, j * P:(j + 1) * P], src, g.ident[:])
                mm.then_inc(tok_turned, 1)
            pe.wait_ge(v_lo, 4)
            pe.wait_ge(v_zero, 2)
            pe.wait_ge(b_lo, 4)
            pe.wait_ge(neg_ok, 1)
            pe.wait_ge(tok_copied, 2)

            def score(r, n):
                gp, ab, half = UNITS[n]
                unit, v, hp, b = NU * r + n, n % 2, (gp * R + r) * 2 + ab, ab * 64
                if n % 4 == 0:
                    pe.wait_ge(q_in[gp], 48 * (r + 1))
                if due(unit - 1):
                    pe.wait_ge(exped, unit - 1)
                for k in range(4):
                    t = 4 * half + k
                    out = ps[:, 2 * v + k // 2, (k % 2) * 256:(k % 2 + 1) * 256]
                    q, keys = slice(t * P, (t + 1) * P), slice(t * P, (t + 2) * P)
                    for x, (qt, kt) in enumerate(((q_h, g.k_h), (q_h, g.k_l), (q_l, g.k_h))):
                        nc.tensor.matmul(out, qt[b:b + 64, gp, q], kt[b:b + 64, gp, keys], start=x == 0, stop=False)
                    if t == 0:
                        nc.tensor.matmul(out[:, 0:P], g.identr[:], negr[:], start=False, stop=False)
                    nc.tensor.matmul(out, g.identr[:], bias_h[:, ds(hp, 1), :].rearrange("p a k -> p (a k)"), start=False, stop=False)
                    mm = nc.tensor.matmul(out, g.identr[:], bias_l[:, ds(hp, 1), :].rearrange("p a k -> p (a k)"),
                                          start=False, stop=True)
                mm.then_inc(scored, 1)

            def turn_and_mix(r, n, ahead):
                gp, ab, half = UNITS[n]
                unit, v = NU * r + n, n % 2
                pe.wait_ge(normed, unit + 1)
                if due(unit):
                    pe.wait_ge(pt_lo, unit)
                for k in range(8):
                    mm = nc.tensor.transpose(ps[:, 4 + k // 4, (k % 4) * P:(k % 4 + 1) * P],
                                             prob[:, v, k * P:(k + 1) * P], g.ident[:])
                mm.then_inc(turned, 1)
                ahead()
                pe.wait_ge(pt_lo, unit + 1)
                if due(unit - 1):
                    pe.wait_ge(gated, unit - 1)
                for k in range(4):
                    for c in range(2):
                        blk = 4 * half + k + c
                        for x, (vt, pt) in enumerate(((v_h, pth), (v_h, ptl), (v_l, pth))):
                            mm = nc.tensor.matmul(ps[:, 6 + v, k * P:(k + 1) * P], vt[:, blk, gp * P:(gp + 1) * P],
                                                  pt[:, (2 * k + c) * P:(2 * k + c + 1) * P],
                                                  start=c == 0 and x == 0, stop=c == 1 and x == 2)
                mm.then_inc(mixed, 1)

            order(pe, score, turn_and_mix)


def phase_swa_samples(nc, a, g):
    ps = g.ps
    with ExitStack() as st:
        def sb(name, shape, dt=F32):
            return st.enter_context(nc.sbuf_tensor(name, shape, dt))

        def sem(name):
            return st.enter_context(nc.semaphore(name))

        ks, vs = sb("t_ks", [P, DEC, 256]), sb("t_vs", [P, DEC, 256])
        kst = sb("t_kst", [P, DEC, 2, P])
        sc_t, sc, pt = sb("t_sc_t", [P, P]), sb("t_sc", [P, P]), sb("t_pt", [P, P])
        bias = sb("t_bias", [P, P])
        sink = sb("t_sink", [P, 1])
        stat = sb("t_stat", [P, 6])
        ov = sb("t_ov", [P, 8, DEC])
        old_in, row_in, out = sem("t_old_in"), sem("t_row_in"), sem("t_out")
        k_turned, k_copied, scored, s_copied, s_turned, biased = (sem(n) for n in (
            "t_k_turned", "t_k_copied", "t_scored", "t_s_copied", "t_s_turned", "t_biased"))
        chain, exped, p_turned, p_copied, mixed, gated, y_hi, y_lo = (sem(n) for n in (
            "t_chain", "t_exped", "t_p_turned", "t_p_copied", "t_mixed", "t_gated", "t_y_hi", "t_y_lo"))
        block = st.enter_context(nc.Block())

        @block.sync
        def _(sp):
            for dst, name in ((ks, "state_swa_k"), (vs, "state_swa_v")):
                nc.sync.dma_start(dst[0:P - 1], a[name][0, :, 1:P].rearrange("b t h d -> t b (h d)")).then_inc(old_in, 16)
            nc.sync.dma_start(ks[P - 1:P], g.kvs_dram[:, 0:256].rearrange("(o b) c -> o b c", o=1)).then_inc(row_in, 16)
            nc.sync.dma_start(vs[P - 1:P], g.kvs_dram[:, 256:512].rearrange("(o b) c -> o b c", o=1)).then_inc(row_in, 16)
            nc.sync.dma_start(bias[:], a["swa_bias_s"]).then_inc(row_in, 16)
            nc.sync.dma_start(sink[:], a["sinks_s"]).then_inc(row_in, 16)
            sp.wait_ge(old_in, 32)
            sp.wait_ge(row_in, 64)
            for src, name in ((ks, "new_swa_k_sample"), (vs, "new_swa_v_sample")):
                nc.sync.dma_start(a[name][0].rearrange("b t h d -> t b (h d)"), src[:]).then_inc(out, 16)
            sp.wait_ge(out, 32)

        @block.scalar
        def _(act):
            for c in range(4):
                act.wait_ge(k_turned, c + 1)
                nc.scalar.activation(kst[:, 2 * c:2 * c + 2].rearrange("p b g k -> p (b g k)"), ps[:, c, :], ACT.Copy).then_inc(k_copied, 1)
            act.wait_ge(scored, 1)
            for ab in range(2):
                nc.scalar.activation(sc_t[:].rearrange("p (c e) -> p c e", e=2)[:, :, ab],
                                     ps[:, 4 + ab, 0:P].rearrange("p (c e) -> p c e", e=2)[:, :, ab], ACT.Copy
                                     ).then_inc(s_copied, 1)
            act.wait_ge(chain, 2)
            nc.scalar.activation(sc[:], sc[:], ACT.Exp, bias=stat[:, 0:1], accum_out=stat[:, 1:2])
            nc.scalar.activation(stat[:, 2:3], stat[:, 0:1], ACT.Exp, bias=sink[:]).then_inc(exped, 1)
            act.wait_ge(p_turned, 1)
            nc.scalar.activation(pt[:], ps[:, 6, 0:P], ACT.Copy).then_inc(p_copied, 1)
            act.wait_ge(gated, 2)
            nc.scalar.activation(g.xh[:, :, SEQ:TOK], ov[:], ACT.Copy).then_inc(y_hi, 1)

        @block.vector
        def _(dve):
            dve.wait_ge(s_turned, 1)
            dve.wait_ge(row_in, 64)
            nc.vector.tensor_tensor(sc[:], ps[:, 0, 0:P], bias[:], ALU.add).then_inc(biased, 1)
            dve.wait_ge(biased, 1)
            nc.vector.tensor_reduce(stat[:, 5:6], sc[:], AX.X, ALU.max, negate=True).then_inc(chain, 1)
            dve.wait_ge(chain, 1)
            nc.vector.tensor_scalar(stat[:, 4:5], sink[:], -1.0, None, ALU.mult).then_inc(biased, 1)
            dve.wait_ge(biased, 2)
            nc.vector.tensor_tensor(stat[:, 0:1], stat[:, 5:6], stat[:, 4:5], ALU.min).then_inc(chain, 1)
            dve.wait_ge(exped, 1)
            nc.vector.tensor_tensor(stat[:, 1:2], stat[:, 1:2], stat[:, 2:3], ALU.add).then_inc(chain, 1)
            dve.wait_ge(chain, 3)
            nc.vector.reciprocal(stat[:, 3:4], stat[:, 1:2]).then_inc(chain, 1)
            dve.wait_ge(chain, 4)
            nc.vector.tensor_scalar(sc[:], sc[:], stat[:, 3:4], None, ALU.mult).then_inc(chain, 1)
            dve.wait_ge(mixed, 1)
            for ab in range(2):
                r = slice(ab * 64, ab * 64 + 64)
                nc.vector.tensor_tensor(ov[r], ps[r, 7, 0:P].rearrange("p (b q e) -> p q b e", b=DEC, e=2)[:, :, :, ab],
                                        g.sgate_s[r], ALU.mult).then_inc(gated, 1)
            dve.wait_ge(y_hi, 1)
            nc.vector.tensor_tensor(g.xl[:, :, SEQ:TOK], ov[:], g.xh[:, :, SEQ:TOK].bitcast(F32), ALU.subtract).then_inc(y_lo, 1)

        @block.tensor
        def _(pe):
            pe.wait_ge(old_in, 32)
            pe.wait_ge(row_in, 64)
            for c in range(4):
                for b in range(2):
                    for gp in range(2):
                        mm = nc.tensor.transpose(ps[:, c, (2 * b + gp) * P:(2 * b + gp + 1) * P],
                                                 ks[:, 2 * c + b, gp * P:(gp + 1) * P], g.ident[:])
                mm.then_inc(k_turned, 1)
            pe.wait_ge(k_copied, 4)
            for b in range(DEC):
                for gp in range(2):
                    for ab in range(2):
                        r = slice(ab * 64, ab * 64 + 64)
                        mm = nc.tensor.matmul(ps[:, 4 + ab, b * H + gp * 8 + ab:b * H + gp * 8 + 8:2], kst[r, b, gp, :],
                                              g.q_s[r, gp * 4:gp * 4 + 4, b], start=True, stop=True)
            pe.drain().then_inc(scored, 1)
            pe.wait_ge(s_copied, 2)
            nc.tensor.transpose(ps[:, 0, 0:P], sc_t[:], g.ident[:]).then_inc(s_turned, 1)
            pe.wait_ge(chain, 5)
            nc.tensor.transpose(ps[:, 6, 0:P], sc[:], g.ident[:]).then_inc(p_turned, 1)
            pe.wait_ge(p_copied, 1)
            for b in range(DEC):
                for gp in range(2):
                    c = b * H + gp * 8
                    mm = nc.tensor.matmul(ps[:, 7, c:c + 8], vs[:, b, gp * P:(gp + 1) * P], pt[:, c:c + 8],
                                          start=True, stop=True)
            mm.then_inc(mixed, 1)


def clear_semaphores(nc, first):
    with nc.Block() as block:
        @block.gpsimd
        def _(pool):
            pool.sem_clear(range(first, 256))


class Globals:
    pass


def program(nc, a):
    g = Globals()
    with ExitStack() as ctx:
        g.o_out = [ctx.enter_context(nc.semaphore(f"o_out{u}")) for u in range(2)]
        g.xo_in = ctx.enter_context(nc.semaphore("xo_in"))
        g.key_in = [ctx.enter_context(nc.semaphore(f"key_in{s}")) for s in range(SLOTS)]
        first_sem = min(nc.free_semaphores)
        def sb(st, name, shape, dt=F32):
            return st.enter_context(nc.sbuf_tensor(name, shape, dt))

        def scratch(name, shape, dt=F32):
            return nc.dram_tensor(name, shape, dt, kind="Internal").ap()

        g.ps = ctx.enter_context(nc.psum_tensor("ps", [P, 8, 512], F32))
        g.gate_dram = scratch("gate_scratch", [H, P, SEQ])
        g.oh_dram, g.ol_dram = scratch("oh_scratch", [H, P, SEQ]), scratch("ol_scratch", [H, P, SEQ])
        g.h1_dram = scratch("h1_scratch", [TOK, D])
        g.qh_dram, g.ql_dram = scratch("qh_scratch", [8, P, SEQ]), scratch("ql_scratch", [8, P, SEQ])
        g.sgate_dram = scratch("sgate_scratch", [8, P, SEQ])
        g.kvs_dram = scratch("kvs_scratch", [DEC, 512])
        g.ident, g.identr, g.ones = sb(ctx, "ident", [P, P]), sb(ctx, "identr", [P, P], R32), sb(ctx, "ones", [P, P])
        g.eps = sb(ctx, "eps", [P, 1])
        g.gains = sb(ctx, "gains", [P, 22])
        with ExitStack() as layer:
            g.gate_s = sb(layer, "gate_s", [P, H, DEC])
            g.qs_nope = sb(layer, "qs_nope", [P, H + 1, DEC])
            g.qs_rope = sb(layer, "qs_rope", [ROPE, H + 1, DEC])
            g.ckv_s = sb(layer, "ckv_s", [P, 3, DEC])
            with ExitStack() as st:
                g.cs = sb(st, "cs", [P, TOK])
                over = nc.sbuf_base
                g.cqh, g.cql = sb(st, "cqh", [P, 4, TOK], R32), sb(st, "cql", [P, 4, TOK], R32)
                g.cq_alias = nc.alloc_sbuf_tensor_at("cq_alias", [P, 8 * TOK], F32, offset=over)
                g.ckvh, g.ckvl = sb(st, "ckvh", [P, 2, SEQ], R32), sb(st, "ckvl", [P, 2, SEQ], R32)
                g.krh = sb(st, "krh", [P, SEQ], R32)
                g.krl = sb(st, "krl", [ROPE, SEQ], R32)
                phase_mla_in(nc, a, g)
                phase_mla_heads(nc, a, g)
            g.mt = nc.alloc_sbuf_tensor_at("mt", [P, KT, TOK], F32, offset=(nc.sbuf_usable_end - KT * TOK * 4) // 64 * 64)
            with ExitStack() as st:
                g.xo_h = sb(st, "xo_h", [P, H, TOK], R32)
                g.xo_l = nc.alloc_sbuf_tensor_at("xo_l", [P, H, TOK], R32, offset=nc.sbuf_base)
                phase_mla_samples(nc, a, g)
                sb(st, "xo_l_room", [P, H, TOK])
                phase_out(nc, a, g, "d", B_MO, g.xo_h, g.xo_l, 2)
        clear_semaphores(nc, first_sem)
        with ExitStack() as layer:
            g.k_h, g.k_l = sb(layer, "k_h", [P, 2, P + SEQ], R32), sb(layer, "k_l", [P, 2, P + SEQ], R32)
            g.kT, g.vT = sb(layer, "kT", [P, 2, TOK]), sb(layer, "vT", [P, 2, TOK])
            g.q_s, g.sgate_s = sb(layer, "q_s", [P, 8, DEC]), sb(layer, "sgate_s", [P, 8, DEC])
            g.sinks, g.nsinks = sb(layer, "sinks", [P, H]), sb(layer, "nsinks", [P, H])
            g.xh, g.xl = sb(layer, "xh", [P, KT, TOK], R32), sb(layer, "xl", [P, KT, TOK], R32)
            phase_norms(nc, a, g, 0)
            phase_swa_in(nc, a, g)
            phase_swa_attention(nc, a, g)
            phase_swa_samples(nc, a, g)
            phase_out(nc, a, g, "h", B_SO, g.xh, g.xl, 1)
            phase_norms(nc, a, g, 1)


_OUTS = [("y_prompt", (1, SEQ, D)), ("y_sample", (DEC, 1, D)), ("new_ckv_prompt", (1, 1, SEQ, KVL)),
         ("new_kpe_prompt", (1, 1, SEQ, ROPE)), ("new_ckv_sample", (1, DEC, 1, KVL)),
         ("new_kpe_sample", (1, DEC, 1, ROPE)), ("new_swa_k_prompt", (1, 1, P, 4, 64)),
         ("new_swa_v_prompt", (1, 1, P, 4, 64)), ("new_swa_k_sample", (1, DEC, P, 4, 64)),
         ("new_swa_v_sample", (1, DEC, P, 4, 64))]


def layouts(np, x):
    def tiles(w):
        rows, cols = w.shape
        return w.reshape(rows // D, KT, P, cols // P, P).transpose(3, 0, 2, 1, 4).reshape(-1, P, D)

    def rows(w, k):
        return w.reshape(k, P, -1).transpose(1, 0, 2).reshape(P, -1)

    w_in = x["mla_w_in"][0]
    key, latent = w_in[:, QL + KVL:QL + KVL + ROPE], w_in[:, :QL + KVL]
    swap = np.r_[ROPE // 2:ROPE, 0:ROPE // 2]
    w_in = np.concatenate([latent, key, key[:, swap], w_in[:, QL + KVL + ROPE:]], axis=1)
    heads = np.array([(2 * gp + ab) * 4 + r for gp in range(2) for r in range(4) for ab in range(2)])
    cols = (heads[:, None] * 64 + np.arange(64)[None, :]).reshape(-1)
    s_in = x["swa_w_in"][0]
    s_in = np.concatenate([s_in[:, cols], s_in[:, D:D + 512], s_in[:, D + 512 + cols]], axis=1)
    w_tiles = np.concatenate([tiles(w_in), tiles(x["mla_w_o"][0]), tiles(s_in), tiles(x["swa_w_o"][0][cols])])
    head_w = []
    for h in list(range(H)) + [H - 1]:
        q = x["mla_w_qb"][0][:, h, :]
        q = np.concatenate([q, q[:, NOPE:][:, swap]], axis=1)
        head_w.append(np.concatenate([rows(q, 4), rows(x["mla_w_uk"][0][:, h, :], 2), rows(x["mla_w_uv"][0][:, h, :], 2)], axis=1))
    pos = np.concatenate([np.arange(SEQ), np.full(DEC, PAST)]).astype(np.float32)
    inv = np.float32(10000.0) ** (-np.arange(0, ROPE, 2, dtype=np.float32) / np.float32(ROPE))
    ang = (pos[:, None] * inv[None, :]).astype(np.float32)
    ang = np.concatenate([ang, ang], axis=1).T
    sign = np.where(np.arange(ROPE) < ROPE // 2, -1, 1).astype(np.float32)[:, None]
    slope = (2.0 ** (-8.0 * (heads + 1) / H)).astype(np.float32)
    q, k = np.arange(P)[:, None], np.arange(2 * P)[None, :]
    dist = (P + q - k).astype(np.float32)
    bias = np.where((dist >= 0) & (dist < P), -slope[:, None, None] * dist, np.float32(-1e30)).astype(np.float32)
    near = (P - 1 - np.arange(P)).astype(np.float32)
    sinks = x["swa_sinks"][0][heads]
    return {
        "x_prompt": x["x_prompt"][0], "x_sample": x["x_sample"][:, 0],
        "cache_ckv": x["cache_ckv"], "cache_kpe": x["cache_kpe"], "page_table": x["page_table"],
        "state_swa_k": x["state_swa_k"], "state_swa_v": x["state_swa_v"],
        "w_tiles": w_tiles, "head_w": np.stack(head_w),
        "w_uk_turned": x["mla_w_uk"][0].transpose(1, 2, 0),
        "w_uv_heads": np.stack([rows(x["mla_w_uv"][0][:, h, :], 2) for h in range(H)]),
        "gains": np.concatenate([x["pre_norm"][0].reshape(KT, P).T, x["pre_norm"][1].reshape(KT, P).T,
                                 x["mla_q_norm"][0].reshape(4, P).T, x["mla_kv_norm"][0].reshape(2, P).T], axis=1),
        "post_gain": np.repeat(x["post_norm"][:, None, :], P, axis=1),
        "sinks": np.repeat(sinks[None, :], P, axis=0), "sinks_s": np.tile(sinks, DEC)[:, None],
        "ident": np.eye(P, dtype=np.float32),
        "mask": np.where(q >= k[:, :P], 0, -1e30).astype(np.float32),
        "never": np.full((P, P), -1e30, np.float32),
        "cs": np.concatenate([np.cos(ang), np.sin(ang) * sign], axis=0).astype(np.float32),
        "swa_bias": bias.transpose(1, 0, 2).reshape(P, -1),
        "swa_bias_s": np.tile(-slope[:, None] * near[None, :], (DEC, 1)).astype(np.float32),
    }


def kernel(**inputs):
    import numpy as _np
    import concourse.bacc as _bacc
    from concourse import mybir as _mybir
    from concourse.bass_utils import run_bass_kernel_spmd as _run

    nc = _bacc.Bacc("TRN2", target_bir_lowering=False, num_devices=1)
    arrays, a = {}, {}
    for name, value in layouts(_np, {n: _np.asarray(v) for n, v in inputs.items()}).items():
        value = _np.ascontiguousarray(value)
        arrays[f"in_{name}"] = value
        a[name] = nc.dram_tensor(f"in_{name}", value.shape, _mybir.dt.from_np(value.dtype), kind="ExternalInput").ap()
    for name, shape in _OUTS:
        a[name] = nc.dram_tensor(f"out_{name}", shape, F32, kind="ExternalOutput").ap()
    program(nc, a)
    r = _run(nc, [arrays], core_ids=[0])
    return tuple(r.results[0][f"out_{name}"] for name, _ in _OUTS)
```
